# Optimizing a Trainium2 kernel written in Bass

```python
import math
import jax, jax.numpy as jnp
from jax import lax
import numpy as np

D_MODEL = 1024
BATCH = 1
SEQ = 256
DEPTH = 1

N_MIXERS = 2
EPS = 1e-5
CONV_WIDTH = 31
CONF_INNER = D_MODEL
SSM_EXPAND = 2
D_INNER = SSM_EXPAND * D_MODEL
SSM_HEAD_DIM = 64
SSM_HEADS = D_INNER // SSM_HEAD_DIM
SSM_GROUPS = 8
SSM_STATE = 128
SSM_CONV = 4
SSD_CHUNK = 128
SSM_CONV_DIM = D_INNER + 2 * SSM_GROUPS * SSM_STATE
SSM_IN_WIDTH = 2 * D_INNER + 2 * SSM_GROUPS * SSM_STATE + SSM_HEADS
N_EXPERTS = 32
TOP_K = 4
D_FF = D_MODEL
SWIGLU_LIMIT = 7.0
SWIGLU_ALPHA = 1.702
MOE_BLOCK = 256

kernel_name = 'hybrid_conformer_mamba2_moe_adaln'

def rmsnorm(x, g):
    xf = x.astype(jnp.float32)
    y = xf * lax.rsqrt(jnp.mean(xf * xf, axis=-1, keepdims=True) + EPS) * g.astype(jnp.float32)
    return y.astype(x.dtype)

def layernorm(x, g, b):
    xf = x.astype(jnp.float32)
    mu = jnp.mean(xf, axis=-1, keepdims=True)
    var = jnp.mean(jnp.square(xf - mu), axis=-1, keepdims=True)
    y = (xf - mu) * lax.rsqrt(var + EPS) * g.astype(jnp.float32) + b.astype(jnp.float32)
    return y.astype(x.dtype)

def modulate(h, shift, scale):
    return h * (1 + scale[:, None, :]) + shift[:, None, :]

def causal_depthwise_conv(u, w, b):
    width, ch = w.shape
    out = lax.conv_general_dilated(
        u, w[:, None, :].astype(u.dtype), window_strides=(1,), padding=[(width - 1, 0)],
        dimension_numbers=('NWC', 'WIO', 'NWC'), feature_group_count=ch)
    return out + b

def conformer_conv_module(h, pw1_w, pw1_b, dw_w, dw_b, ln_g, ln_b, pw2_w, pw2_b):
    u = h @ pw1_w + pw1_b
    a, gt = jnp.split(u, 2, axis=-1)
    u = a * jax.nn.sigmoid(gt)
    u = causal_depthwise_conv(u, dw_w, dw_b)
    u = layernorm(u, ln_g, ln_b)
    u = jax.nn.silu(u)
    return u @ pw2_w + pw2_b

def ssd_chunked_scan(x, dt, A, Bm, Cm):
    bsz, s, nh, p = x.shape
    g, n = Bm.shape[-2:]
    hg = nh // g
    L = SSD_CHUNK
    nc = s // L

    def chunks(t):
        return jnp.moveaxis(t.reshape((bsz, nc, L) + t.shape[2:]), 1, 0)

    xc = chunks(x.reshape(bsz, s, g, hg, p))
    dtc = chunks(dt.reshape(bsz, s, g, hg))
    ac = dtc * A.reshape(g, hg)
    bc = chunks(Bm)
    cc = chunks(Cm)
    causal = jnp.tril(jnp.ones((L, L), dtype=bool))

    def step(state, inp):
        xk, dtk, ak, bk, ck = inp
        cum = jnp.cumsum(ak, axis=1)
        seg = cum[:, :, None] - cum[:, None, :]
        decay = jnp.exp(jnp.where(causal[None, :, :, None, None], seg, -jnp.inf))
        cb = jnp.einsum('blgn,bsgn->blsg', ck, bk)
        w = cb[..., None] * decay * dtk[:, None]
        y_diag = jnp.einsum('blsgh,bsghp->blghp', w, xk)
        y_off = jnp.einsum('blgn,bghpn->blghp', ck, state) * jnp.exp(cum)[..., None]
        to_end = jnp.exp(cum[:, -1:] - cum) * dtk
        new_state = (state * jnp.exp(cum[:, -1])[..., None, None]
                     + jnp.einsum('bsgn,bsgh,bsghp->bghpn', bk, to_end, xk))
        return new_state, y_diag + y_off

    state0 = jnp.zeros((bsz, g, hg, p, n), jnp.float32)
    _, ys = lax.scan(step, state0, (xc, dtc, ac, bc, cc))
    return jnp.moveaxis(ys, 0, 1).reshape(bsz, s, nh, p)

def mamba2_mixer(h, in_w, conv_w, conv_b, dt_bias, a_log, d_skip, norm_g, out_w):
    bsz, s, _ = h.shape
    zxbcdt = h @ in_w
    z = zxbcdt[..., :D_INNER]
    xbc = zxbcdt[..., D_INNER:D_INNER + SSM_CONV_DIM]
    dt = zxbcdt[..., D_INNER + SSM_CONV_DIM:]
    xbc = jax.nn.silu(causal_depthwise_conv(xbc, conv_w, conv_b))
    xs = xbc[..., :D_INNER].astype(jnp.float32).reshape(bsz, s, SSM_HEADS, SSM_HEAD_DIM)
    bm = xbc[..., D_INNER:D_INNER + SSM_GROUPS * SSM_STATE].astype(jnp.float32).reshape(bsz, s, SSM_GROUPS, SSM_STATE)
    cm = xbc[..., D_INNER + SSM_GROUPS * SSM_STATE:].astype(jnp.float32).reshape(bsz, s, SSM_GROUPS, SSM_STATE)
    dt = jax.nn.softplus(dt.astype(jnp.float32) + dt_bias.astype(jnp.float32))
    A = -jnp.exp(a_log.astype(jnp.float32))
    y = ssd_chunked_scan(xs, dt, A, bm, cm)
    y = y + d_skip.astype(jnp.float32)[:, None] * xs
    y = y.reshape(bsz, s, D_INNER) * jax.nn.silu(z.astype(jnp.float32))
    yg = y.reshape(bsz, s, SSM_GROUPS, D_INNER // SSM_GROUPS)
    yg = yg * lax.rsqrt(jnp.mean(yg * yg, axis=-1, keepdims=True) + EPS)
    y = yg.reshape(bsz, s, D_INNER) * norm_g.astype(jnp.float32)
    return y.astype(h.dtype) @ out_w

def moe_ffn(h, router_w, router_b, w1, b1, w2, b2):
    bsz, s, d = h.shape
    t = bsz * s
    hf = h.reshape(t, d)
    logits = (hf @ router_w + router_b).astype(jnp.float32)
    top_val, top_idx = lax.top_k(logits, TOP_K)
    gate = jax.nn.softmax(top_val, axis=-1)
    n_assign = t * TOP_K
    flat_e = top_idx.reshape(-1)
    flat_tok = jnp.arange(n_assign, dtype=jnp.int32) // TOP_K
    order = jnp.argsort(flat_e)
    sorted_e = flat_e[order]
    counts = jnp.bincount(flat_e, length=N_EXPERTS)
    padded = ((counts + MOE_BLOCK - 1) // MOE_BLOCK) * MOE_BLOCK
    start = jnp.cumsum(counts) - counts
    ends = jnp.cumsum(padded)
    pstart = ends - padded
    dest = pstart[sorted_e] + (jnp.arange(n_assign, dtype=jnp.int32) - start[sorted_e])
    n_slots = n_assign + N_EXPERTS * MOE_BLOCK
    n_blocks = n_slots // MOE_BLOCK
    slot_tok = jnp.full((n_slots,), t, dtype=jnp.int32).at[dest].set(flat_tok[order])
    slot_gate = jnp.zeros((n_slots,), jnp.float32).at[dest].set(gate.reshape(-1)[order])
    block_e = jnp.minimum(
        jnp.searchsorted(ends, jnp.arange(n_blocks, dtype=jnp.int32) * MOE_BLOCK, side='right'),
        N_EXPERTS - 1)
    xb = jnp.take(hf, slot_tok, axis=0, mode='fill', fill_value=0).reshape(n_blocks, MOE_BLOCK, d)

    def expert_block(args):
        xk, e = args
        gu = xk @ w1[e] + b1[e]
        g_lin, u_lin = gu[:, :D_FF], gu[:, D_FF:]
        g_lin = jnp.minimum(g_lin, SWIGLU_LIMIT)
        u_lin = jnp.clip(u_lin, -SWIGLU_LIMIT, SWIGLU_LIMIT)
        act = (u_lin + 1) * (g_lin * jax.nn.sigmoid(SWIGLU_ALPHA * g_lin))
        return act @ w2[e] + b2[e]

    ys = lax.map(expert_block, (xb, block_e)).reshape(n_slots, d)
    out = jnp.zeros((t, d), ys.dtype).at[slot_tok].add(ys * slot_gate[:, None].astype(ys.dtype), mode='drop')
    return out.reshape(bsz, s, d)

def setup_inputs(seed: int = 0) -> dict:
    key = jax.random.key(seed)
    ks = jax.random.split(key, 32)
    f32 = jnp.float32
    D = D_MODEL
    n_a = (DEPTH + N_MIXERS - 1) // N_MIXERS
    n_b = DEPTH // N_MIXERS

    def nrm(k, shape, scale):
        return jax.random.normal(k, shape, f32) * scale

    dt_u = jax.random.uniform(ks[18], (n_b, SSM_HEADS), f32)
    dt0 = jnp.exp(dt_u * (math.log(0.1) - math.log(0.001)) + math.log(0.001))
    return {
        'x': nrm(ks[0], (BATCH, SEQ, D), 1.0),
        'c': nrm(ks[1], (BATCH, D), 1.0),
        'ada_w': nrm(ks[2], (DEPTH, D, 6 * D), 0.02),
        'ada_b': nrm(ks[3], (DEPTH, 6 * D), 0.02),
        'mix_norm_g': 1.0 + nrm(ks[4], (DEPTH, D), 0.02),
        'ffn_norm_g': 1.0 + nrm(ks[5], (DEPTH, D), 0.02),
        'conf_pw1_w': nrm(ks[6], (n_a, D, 2 * CONF_INNER), D ** -0.5),
        'conf_pw1_b': nrm(ks[7], (n_a, 2 * CONF_INNER), 0.02),
        'conf_dw_w': nrm(ks[8], (n_a, CONV_WIDTH, CONF_INNER), CONV_WIDTH ** -0.5),
        'conf_dw_b': nrm(ks[9], (n_a, CONF_INNER), 0.02),
        'conf_ln_g': 1.0 + nrm(ks[10], (n_a, CONF_INNER), 0.02),
        'conf_ln_b': nrm(ks[11], (n_a, CONF_INNER), 0.02),
        'conf_pw2_w': nrm(ks[12], (n_a, CONF_INNER, D), CONF_INNER ** -0.5),
        'conf_pw2_b': nrm(ks[13], (n_a, D), 0.02),
        'ssm_in_w': nrm(ks[14], (n_b, D, SSM_IN_WIDTH), D ** -0.5),
        'ssm_conv_w': nrm(ks[15], (n_b, SSM_CONV, SSM_CONV_DIM), SSM_CONV ** -0.5),
        'ssm_conv_b': nrm(ks[16], (n_b, SSM_CONV_DIM), 0.02),
        'ssm_dt_bias': dt0 + jnp.log(-jnp.expm1(-dt0)),
        'ssm_a_log': jnp.log(jax.random.uniform(ks[17], (n_b, SSM_HEADS), f32, minval=1.0, maxval=16.0)),
        'ssm_d': 1.0 + nrm(ks[19], (n_b, SSM_HEADS), 0.1),
        'ssm_norm_g': 1.0 + nrm(ks[20], (n_b, D_INNER), 0.02),
        'ssm_out_w': nrm(ks[21], (n_b, D_INNER, D), D_INNER ** -0.5),
        'router_w': nrm(ks[22], (DEPTH, D, N_EXPERTS), D ** -0.5),
        'router_b': nrm(ks[23], (DEPTH, N_EXPERTS), 0.01),
        'exp_w1': nrm(ks[24], (DEPTH, N_EXPERTS, D, 2 * D_FF), D ** -0.5),
        'exp_b1': nrm(ks[25], (DEPTH, N_EXPERTS, 2 * D_FF), 0.02),
        'exp_w2': nrm(ks[26], (DEPTH, N_EXPERTS, D_FF, D), D_FF ** -0.5),
        'exp_b2': nrm(ks[27], (DEPTH, N_EXPERTS, D), 0.02),
        'final_norm_g': 1.0 + nrm(ks[28], (D,), 0.02),
    }

def reference(x, c, ada_w, ada_b, mix_norm_g, ffn_norm_g,
              conf_pw1_w, conf_pw1_b, conf_dw_w, conf_dw_b, conf_ln_g, conf_ln_b, conf_pw2_w, conf_pw2_b,
              ssm_in_w, ssm_conv_w, ssm_conv_b, ssm_dt_bias, ssm_a_log, ssm_d, ssm_norm_g, ssm_out_w,
              router_w, router_b, exp_w1, exp_b1, exp_w2, exp_b2, final_norm_g):
    c_act = jax.nn.silu(c)
    for i in range(DEPTH):
        mod = c_act @ ada_w[i] + ada_b[i]
        sh1, sc1, g1, sh2, sc2, g2 = jnp.split(mod, 6, axis=-1)
        h = modulate(rmsnorm(x, mix_norm_g[i]), sh1, sc1)
        j = i // N_MIXERS
        if i % N_MIXERS == 0:
            y = conformer_conv_module(h, conf_pw1_w[j], conf_pw1_b[j], conf_dw_w[j], conf_dw_b[j],
                                      conf_ln_g[j], conf_ln_b[j], conf_pw2_w[j], conf_pw2_b[j])
        else:
            y = mamba2_mixer(h, ssm_in_w[j], ssm_conv_w[j], ssm_conv_b[j], ssm_dt_bias[j],
                             ssm_a_log[j], ssm_d[j], ssm_norm_g[j], ssm_out_w[j])
        x = x + g1[:, None, :] * y
        h = modulate(rmsnorm(x, ffn_norm_g[i]), sh2, sc2)
        x = x + g2[:, None, :] * moe_ffn(h, router_w[i], router_b[i], exp_w1[i], exp_b1[i], exp_w2[i], exp_b2[i])
    return rmsnorm(x, final_norm_g)


_drawn_inputs = setup_inputs


def setup_inputs(seed=0):
    import zlib

    import numpy as np

    out = dict(_drawn_inputs(seed))
    spreads = {}
    factors = {'mix_norm_g': 4.163,
     'conf_pw1_b': 9.853,
     'conf_dw_b': 3.489,
     'conf_ln_g': 12.207,
     'conf_ln_b': 14.368,
     'conf_pw2_b': 4.416,
     'router_b': 16.965,
     'exp_b1': 8.0,
     'exp_b2': 43.379,
     'final_norm_g': 19.581,
     'ffn_norm_g': 3.845}
    for name, (base, spread) in spreads.items():
        noise = np.random.default_rng([zlib.crc32(name.encode()), seed]).standard_normal(out[name].shape)
        drawn = base * np.exp(spread * noise) if base else spread * noise
        out[name] = __import__('jax').numpy.asarray(drawn.astype(out[name].dtype))
    for name, factor in factors.items():
        out[name] = (out[name] * factor).astype(out[name].dtype)
    return out
```

```python
from contextlib import ExitStack

import concourse.bass as bass
from concourse import mybir

F32 = mybir.dt.float32
BF16 = mybir.dt.bfloat16
I32 = mybir.dt.int32
U32 = mybir.dt.uint32
ALU = mybir.AluOpType
ACT = mybir.ActivationFunctionType
AX = mybir.AxisListType

P = 128
EPS = 1e-5
LIMIT = 7.0
ALPHA = 1.702
TOP_K = 4
SLOTS = 64
RING = 16
UNROLL = 4
PE_TAPS = 6
DIAGS = 2 * PE_TAPS


def build_trunk(nc, x, c, ada_w, ada_b, mix_g, ffn_g, pw1_w, pw1_b, dw_w, dw_b, ln_g, ln_b,
                pw2_w, pw2_b, router_w, router_b, exp_w1, exp_b1, exp_w2, exp_b2, final_g, out,
                capacity=SLOTS):
    T, D = x.shape[1], x.shape[2]
    E = router_w.shape[2]
    F = exp_w2.shape[2]
    TAPS = dw_w.shape[1]
    PAD = TAPS - 1
    KT = D // P
    TT = T // P
    H = F // 2
    NB = T // SLOTS
    CAND = E * (NB - 1)
    EXTRA = 16
    NCH = 12
    GROUPS = 3
    stream = [("ada", k) for k in range(KT)]
    for t in range(KT):
        stream += [("pw1", t), ("ada", KT + 2 * t), ("ada", KT + 2 * t + 1)]
    stream += [("pw2", q) for q in range(4)]
    number = {what: n for n, what in enumerate(stream)}
    CH_EXP = len(stream)
    ITEMS = E + EXTRA
    assert CAND == 96 and E == 32 and T == 256 and D == 1024 and (UNROLL * NCH) % RING == 0

    ctx = ExitStack()
    with ctx:
        def sb(name, shape, dt=F32):
            return ctx.enter_context(nc.sbuf_tensor(name, shape, dt))

        def sem(name):
            return ctx.enter_context(nc.semaphore(name))

        ring = sb("ring", [P, RING, 2048])
        xT = sb("xT", [P, KT, T])
        hT = sb("hT", [P, KT, T])
        acc = sb("acc", [P, TT, D])
        arena = sb("arena", [P, KT * (PAD + T) + KT * T])
        upad = arena[:, 0:KT * (PAD + T)].rearrange("p (k s) -> p k s", k=KT)
        conv = arena[:, KT * (PAD + T):].rearrange("p (k s) -> p k s", k=KT)
        hsplit = arena[:, 0:3 * TT * D // 2].bitcast(BF16).rearrange("p (a t d) -> p a t d", a=3, t=TT)
        scratch = sb("scratch", [P, KT, T])
        flat = scratch[:, :, :].rearrange("p k s -> p (k s)")
        diag = flat[:, 0:DIAGS * P].rearrange("p (n c) -> p n c", n=DIAGS)
        convb = flat[:, DIAGS * P:DIAGS * P + T]
        g_lim, u_lim, sig, act = (flat[:, n * H:(n + 1) * H] for n in range(4))
        b2g = flat[0:E, 0:D]
        rest = [flat[:, (2 + n) * H:(3 + n) * H] for n in range(2)]
        glu = sb("glu", [P, 2, T])
        onehot = sb("onehot", [P, 2, TT, P])
        onehotT = sb("onehotT", [P, 2, TT, P])
        vrow = onehot[:, 0, 0, :]
        root, rstd = (onehotT[:, n, :, :].rearrange("p t c -> p (t c)") for n in range(2))
        vcol = sb("vcol", [P, 120])
        dwcol = sb("dwcol", [P, KT * TAPS])
        xg = sb("xg", [P, 2, KT, SLOTS])
        dwrow = xg[:, :, :, :].rearrange("p a k s -> p (a k s)")[0:TAPS, :]
        actT = sb("actT", [P, 4, P])
        modrow = actT[:, :, :].rearrange("p q c -> p (q c)")
        ysb = sb("ysb", [P, H])
        cact = sb("cact", [P, KT])
        cwide = sb("cwide", [P, KT, 32])
        modcol = sb("modcol", [P, GROUPS, 16])
        a1 = sb("a1", [P, KT])
        a2 = sb("a2", [P, KT])
        g1b = sb("g1b", [P, KT])
        b1s = sb("b1s", [3 * E, 2 * F], BF16)
        g2half = sb("g2half", [P, H])
        rw = sb("rw", [P, KT, E])
        rb = sb("rb", [E, 1])
        ident = sb("ident", [P, P])
        mean_of = sb("mean_of", [P, P])
        ones_bf = sb("ones_bf", [P, P], BF16)
        before = sb("before", [P, P], BF16)
        pick = sb("pick", [P, 2, P])
        iota_s = sb("iota_s", [P, 2, SLOTS])
        iota_e = sb("iota_e", [P, E])
        eps = sb("eps", [P, 1])
        logT = sb("logT", [E, T])
        gateT = logT
        logit = sb("logit", [P, TT, E])
        top = sb("top", [P, TT, 8])
        topi = sb("topi", [P, TT, 8], U32)
        topf = sb("topf", [P, TT, TOP_K])
        negm = sb("negm", [P, TT])
        prob = sb("prob", [P, TT, TOP_K])
        psum4 = sb("psum4", [P, TT])
        rp4 = sb("rp4", [P, TT])
        gatek = sb("gatek", [P, TT, TOP_K])
        hits, gates4 = (flat[:, at:at + TT * TOP_K * E].rearrange("p (t k e) -> p t k e", t=TT, k=TOP_K)
                        for at in (D, D + TT * TOP_K * E))
        mask = sb("mask", [P, TT, E])
        mask_bf = sb("mask_bf", [P, TT, E], BF16)
        most = sb("most", [P, 1])
        flag = sb("flag", [P, 1], I32)
        slot = sb("slot", [P, TT, ITEMS + 1])
        gate = sb("gate", [P, TT, ITEMS + 1])
        bsel = sb("bsel", [3 * E, ITEMS + 1], BF16)
        onehot_bf = sb("onehot_bf", [P, 2, TT, SLOTS], BF16)
        bias_of = sb("bias_of", [3 * E, 2, SLOTS], BF16)
        ssq = sb("ssq", [P, TT])
        fin = sb("fin", [P, TT])
        frstd = sb("frstd", [P, TT])
        m3 = glu[:, :, CAND:CAND + CAND // 2].bitcast(BF16)
        t3 = glu[:, :, 0:CAND].rearrange("p t (b e) -> p t b e", e=E)
        t3T = cwide[0:CAND, :, :].rearrange("p k c -> p (k c)")
        thr = sb("thr", [CAND, 1])
        filled = sb("filled", [CAND, 1])
        filled_bf = sb("filled_bf", [CAND, 1], BF16)
        rank = g1b[0:CAND, 0:1]
        take = sb("take", [CAND, EXTRA])
        take_bf = a1[0:CAND, :].bitcast(BF16)
        rep = glu[0:CAND, 0, 160:160 + CAND // 2].bitcast(BF16).rearrange("p (b e) -> p b e", e=E)
        ecol = glu[0:CAND, 1, 160:160 + E]
        enum = g1b[0:CAND, 1:2]
        eidx = modcol[0:1, 0, :].bitcast(I32)
        fng = xT[:, 0:4, :].rearrange("p k s -> p (k s)")

        bank = [ctx.enter_context(nc.psum_tensor(f"bank{n}", [P, 512], F32)) for n in range(8)]
        G_PS, U_PS, Y_PS, X_PS, A_PS, O_PS = bank[0:6]
        S_PS = bank[6:8]

        s_x, s_vec, s_dw, s_b1 = sem("x_in"), sem("vec_in"), sem("dw_in"), sem("b1_in")
        s_rw, s_g2b, s_fng, s_out = sem("rw_in"), sem("late_in"), sem("fng_in"), sem("out_done")
        landed = [sem(f"landed{n}") for n in range(RING)]
        used = sem("chunks_used")
        s_const, s_const_v = sem("const_ready"), sem("const_v_ready")
        p_vec, p_dw, p_x, v_vec, v_dw = sem("vec_turned"), sem("dw_turned"), sem("x_turned"), sem("vcol_ready"), sem("dwcol_ready")
        v_xa, v_xv, s_sq, p_st, s_root, s_rstd = (sem(n) for n in
            ("xT_by_act", "xT_by_dve", "squares_ready", "stat_ready", "root_ready", "rstd_ready"))
        s_cact, s_cwide, s_b1f, s_acc_free = sem("cact_ready"), sem("cwide_ready"), sem("b1_split"), sem("acc_free")
        s_row, p_row, s_mod, s_h = sem("modrow_ready"), sem("modrow_turned"), sem("mod_ready"), sem("h_ready")
        s_glu, s_u, s_diag, p_taps, s_b2r = (sem(n) for n in
            ("glu_ready", "u_ready", "diag_ready", "taps_done", "b2_taken"))
        s_conv, s_cent, s_silu = sem("conv_ready"), sem("centred"), sem("silu_ready")
        s_nrm = sem("ln_normed")
        p_pw2, s_y2, s_x2, s_n2, s_h2 = sem("pw2_done"), sem("y_scaled"), sem("x2_ready"), sem("x2_normed"), sem("h2_ready")
        p_log, s_logT, p_log2, s_logit = sem("logitsT_done"), sem("logT_ready"), sem("logits_done"), sem("logit_ready")
        p_h2, s_hi, s_rest, s_mid, s_lo = sem("h2_turned"), sem("h_hi"), sem("h_rest"), sem("h_mid"), sem("h_lo")
        s_negm, s_prob, s_mask, p_pos, s_tab = sem("negmax_ready"), sem("prob_ready"), sem("mask_ready"), sem("pos_done"), sem("tables_ready")
        s_gate, p_gT, s_gT, p_g2, s_b2g, p_b2, p_x2, s_x2c = (sem(n) for n in
            ("gate_ready", "gate_turned", "gateT_ready", "g2_spread", "b2g_ready", "b2_done", "x2_turned", "x2_copied"))
        dve = sem("vector_steps")
        pool_s = sem("gpsimd_steps")
        sel_ready, xg_done, xg_ready, oT_done, oT_ready = (sem(n) for n in
            ("select_ready", "gathered", "xg_ready", "onehot_turned", "onehotT_ready"))
        g_clamped, sig_ready, act_ready, aT_done, aT_ready = (sem(n) for n in
            ("g_clamped", "sigmoid_ready", "act_ready", "act_turned", "actT_ready"))
        y_ready, sc_done, acc_done, u_clamped, mid_act = (sem(n) for n in
            ("y_ready", "scattered", "accumulated", "u_clamped", "glu_product"))
        x_p, x_v, x_sp = sem("extra_pe"), sem("extra_dve"), sem("extra_experts")
        s_ssq, s_fr, s_fin, s_ff = sem("sumsq_ready"), sem("final_root"), sem("final_scaled"), sem("final_rstd")

        block = ctx.enter_context(nc.Block())

        C0, MG, FG, PB1, DB, LG, LB, PB2, AB = 0, 8, 16, 24, 40, 48, 56, 64, 72

        def w_slot(n):
            return ring[:, n % RING, :]

        def chunk_in(n):
            return landed[n % RING], 16 * (n // RING + 1)

        @block.sync
        def _(sp):
            def row(v, at, k):
                sp.dma_start(vrow[at:at + k, :], v.rearrange("(r b) -> r b", b=P)).then_inc(s_vec, 16)

            sp.dma_start(acc[:, :, :], x[0].rearrange("(t p) d -> p t d", p=P)).then_inc(s_x, 16)
            row(c[0], C0, 8)
            row(mix_g[0], MG, 8)
            row(ffn_g[0], FG, 8)
            row(pw1_b[0], PB1, 16)
            row(dw_b[0], DB, 8)
            row(ln_g[0], LG, 8)
            row(ln_b[0], LB, 8)
            row(pw2_b[0], PB2, 8)
            row(ada_b[0], AB, 48)
            sp.dma_start(dwrow, dw_w[0]).then_inc(s_dw, 16)
            sp.dma_start(rw[:, :, :], router_w[0].rearrange("(k p) e -> p k e", p=P)).then_inc(s_rw, 16)
            sp.dma_start(rb[:, :], router_b[0].rearrange("(e a) -> e a", a=1)).then_inc(s_rw, 16)

            pw1_v = pw1_w[0].rearrange("(k p) (h n) -> p h k n", p=P, h=2)
            pw2_v = pw2_w[0].rearrange("(k p) n -> p k n", p=P)
            for n, (what, k) in enumerate(stream):
                if n >= RING:
                    sp.wait_ge(used, n - RING + 1)
                dst = w_slot(n)
                if what == "ada":
                    src = ada_w[0, (k % KT) * P:(k % KT + 1) * P, k // KT * 2048:(k // KT + 1) * 2048]
                elif what == "pw1":
                    dst = dst.rearrange("p (h k n) -> p h k n", h=2, k=KT)
                    src = pw1_v[:, :, :, k * P:(k + 1) * P]
                else:
                    dst = dst.rearrange("p (k n) -> p k n", k=KT)
                    src = pw2_v[:, :, k * 256:(k + 1) * 256]
                sp.dma_start(dst, src).then_inc(landed[n % RING], 16)

            w1_rows = exp_w1[0].rearrange("e (k p) n -> e k p n", p=P)
            w2_rows = exp_w2[0].rearrange("e (q a p) n -> e q p a n", p=P, a=2)

            def expert(it, j, e):
                for q in range(NCH):
                    n = CH_EXP + j * NCH + q
                    sp.wait_ge(used, it * (UNROLL * NCH) + (n - RING + 1))
                    if q < KT:
                        sp.dma_start(w_slot(n), w1_rows[bass.ds(e, 1), q, :, :].rearrange("e p n -> (e p) n")
                                     ).then_inc(landed[n % RING], 16)
                    else:
                        sp.dma_start(w_slot(n).rearrange("p (a n) -> p a n", a=2),
                                     w2_rows[bass.ds(e, 1), q - KT, :, :, :].rearrange("e p a n -> (e p) a n")
                                     ).then_inc(landed[n % RING], 16)

            with sp.Fori(0, E // UNROLL) as it:
                for j in range(UNROLL):
                    expert(it, j, it * UNROLL + j)
            sp.wait_ge(s_tab, 1)
            more = sp.value_load(flag[0:1, 0:1], min_val=0, max_val=1)
            with sp.If(more > 0):
                sp.wait_ge(x_sp, 1)
                with sp.Fori(E // UNROLL, ITEMS // UNROLL) as it:
                    for j in range(UNROLL):
                        e = sp.value_load(eidx[0:1, bass.ds(it * UNROLL + (j - E), 1)], min_val=0, max_val=E - 1)
                        expert(it, j, e)
            for t in range(TT):
                sp.wait_ge(s_fin, t + 1)
                sp.dma_start(out[0, t * P:(t + 1) * P, :], acc[:, t, :]).then_inc(s_out, 16)
            sp.wait_ge(s_out, 16 * TT)

        @block.gpsimd
        def _(pool):
            n = [0]

            def step(ins):
                n[0] += 1
                ins.then_inc(pool_s, 1)

            step(pool.memset(ident[:, :], 0.0))
            step(pool.memset(pick[:, :, :], 0.0))
            step(pool.memset(before[:, :], 1.0))
            pool.wait_ge(pool_s, 3)
            pool.affine_select(out=ident[:, :], in_=ident[:, :], compare_op=ALU.not_equal, fill=1.0,
                               base=0, pattern=[[-1, P]], channel_multiplier=1).then_inc(s_const, 1)
            for r in range(2):
                pool.affine_select(out=pick[:, r, :], in_=pick[:, r, :], compare_op=ALU.not_equal, fill=1.0,
                                   base=-(64 + 32 * r), pattern=[[0, P]], channel_multiplier=1).then_inc(s_const, 1)
            pool.affine_select(out=before[:, :], in_=before[:, :], compare_op=ALU.is_gt, fill=0.0,
                               base=0, pattern=[[1, P]], channel_multiplier=-1).then_inc(s_const, 1)
            pool.iota(iota_s[:, :, :], pattern=[[0, 2], [1, SLOTS]], base=0, channel_multiplier=0,
                      allow_small_or_imprecise_dtypes=True).then_inc(s_const, 1)
            pool.iota(iota_e[:, :], pattern=[[1, E]], base=0, channel_multiplier=0,
                      allow_small_or_imprecise_dtypes=True).then_inc(s_const, 1)

            for b in range(4):
                t, d0 = b // 2, (b % 2) * 512
                pool.wait_ge(s_mid, b + 1)
                pool.tensor_tensor(hsplit[:, 2, t, d0:d0 + 512], rest[b % 2], hsplit[:, 1, t, d0:d0 + 512],
                                   ALU.subtract).then_inc(s_lo, 1)

        @block.scalar
        def _(a):
            n = [0]

            def step(ins):
                n[0] += 1
                ins.then_inc(act_s, 1)
                return n[0]

            a.wait_ge(p_vec, 1)
            a.activation(vcol[:, :], bank[0][:, 0:120], ACT.Copy).then_inc(v_vec, 1)
            a.wait_ge(v_vec, 1)
            a.activation(cact[:, :], vcol[:, C0:C0 + KT], ACT.Silu).then_inc(s_cact, 1)
            for b in range(2):
                a.wait_ge(p_x, b + 1)
                a.activation(xT[:, 2 * b:2 * b + 2, :], bank[2 + b][:, :].rearrange("p (k s) -> p k s", k=2),
                             ACT.Copy).then_inc(v_xa, 1)

            def squares(lo, hi, src):
                return a.activation(scratch[:, lo:hi, :], src[:, lo:hi, :], ACT.Square)

            a.wait_ge(v_xa, 2)
            squares(0, 4, xT).then_inc(s_sq, 1)
            a.wait_ge(v_xv, 2)
            squares(4, 8, xT).then_inc(s_sq, 1)

            def sqrt(k, b):
                a.wait_ge(p_st, k)
                a.wait_ge(s_const_v, 1)
                a.activation(root, bank[b][:, 0:T], ACT.Sqrt, bias=eps[:, 0:1]).then_inc(s_root, 1)

            sqrt(1, 6)
            a.wait_ge(p_x, 4)
            a.dma_start(acc[0:E, :, :].rearrange("p t d -> p (t d)"), exp_b1[0]).then_inc(s_b1, 16)

            def modrow_out(g):
                a.wait_ge(used, number["ada", g * KT + KT - 1] + 1)
                if g:
                    a.wait_ge(p_row, g)
                a.activation(modrow, bank[7][:, :], ACT.Copy).then_inc(s_row, 1)

            modrow_out(0)
            a.wait_ge(s_b1f, 5)
            a.dma_start(acc[:, 0, :], ada_b[0, 5 * D:6 * D].partition_broadcast(P)).then_inc(s_g2b, 16)
            a.dma_start(acc[0:E, 1, :], exp_b2[0]).then_inc(s_g2b, 16)

            def diagonals(t):
                if t >= 2:
                    a.wait_ge(p_taps, t - 1)
                for m in range(PE_TAPS):
                    s = (t % 2) * PE_TAPS + m
                    a.activation(diag[:, s, :], ident[:, :], ACT.Copy,
                                 scale=dwcol[:, t * TAPS + m:t * TAPS + m + 1]).then_inc(s_diag, 1)

            a.wait_ge(v_dw, 1)
            a.wait_ge(s_b1f, 5)
            diagonals(0)
            for t in range(KT):
                a.wait_ge(used, number["pw1", t] + 1)
                if t >= 2:
                    a.wait_ge(s_u, t - 1)
                a.activation(glu[:, t % 2, :], bank[1 + t % 2][:, T:2 * T], ACT.Sigmoid,
                             bias=vcol[:, PB1 + 8 + t:PB1 + 9 + t]).then_inc(s_glu, 1)
                if t + 1 < KT:
                    diagonals(t + 1)
                if t == 3:
                    modrow_out(1)
            modrow_out(2)

            a.wait_ge(p_taps, KT)
            for q in range(4):
                a.wait_ge(s_cent, q + 1)
                squares(2 * q, 2 * q + 2, conv).then_inc(s_sq, 1)
            sqrt(3, 6)
            for k in range(KT):
                a.wait_ge(s_nrm, k // 2 + 1)
                a.activation(conv[:, k, :], conv[:, k, :], ACT.Silu, scale=vcol[:, LG + k:LG + k + 1],
                             bias=vcol[:, LB + k:LB + k + 1]).then_inc(s_silu, 1)
            for m in range(KT):
                a.wait_ge(p_pw2, m // 2 + 1) if m % 2 == 0 else a.wait_ge(used, number["pw2", m // 2] + 1)
                if m == 0:
                    a.wait_ge(s_mod, 3)
                if m >= 2:
                    a.wait_ge(s_x2, m - 1)
                a.activation(glu[:, m % 2, :], bank[1 + m % 4][:, 0:T], ACT.Identity,
                             scale=modcol[:, 1, m:m + 1], bias=g1b[:, m:m + 1]).then_inc(s_y2, 1)
                if m >= 1:
                    a.wait_ge(s_x2, m)
                    squares(m - 1, m, xT).then_inc(s_sq, 1)
            a.wait_ge(s_x2, KT)
            squares(KT - 1, KT, xT).then_inc(s_sq, 1)
            sqrt(4, 5)
            for k in range(0, KT, 2):
                a.wait_ge(s_n2, k // 2 + 1)
                a.activation(hT[:, k, :], hT[:, k, :], ACT.Identity, scale=a2[:, k:k + 1],
                             bias=modcol[:, 1, 8 + k:9 + k]).then_inc(s_h2, 1)
            a.wait_ge(s_b2g, 1)
            for b in range(4):
                t, d0 = b // 2, (b % 2) * 512
                a.wait_ge(p_x2, b + 1)
                a.activation(acc[:, t, d0:d0 + 512], bank[1 + b][:, :], ACT.Copy).then_inc(s_x2c, 1)
            a.dma_start(fng, final_g.partition_broadcast(P)).then_inc(s_fng, 16)
            a.wait_ge(s_negm, 1)
            for t in range(TT):
                a.activation(prob[:, t, :], top[:, t, 0:TOP_K], ACT.Exp, bias=negm[:, t:t + 1],
                             accum_out=psum4[:, t:t + 1]).then_inc(s_prob, 1)
            for b in range(4):
                t, d0 = b // 2, (b % 2) * 512
                a.wait_ge(p_h2, b + 1)
                a.activation(hsplit[:, 0, t, d0:d0 + 512], bank[1 + b][:, :], ACT.Copy).then_inc(s_hi, 1)
                a.wait_ge(s_rest, b + 1)
                a.activation(hsplit[:, 1, t, d0:d0 + 512], rest[b % 2], ACT.Copy).then_inc(s_mid, 1)
            def xg_out(cnt, b):
                a.wait_ge(xg_done, cnt)
                a.activation(xg[:, b, :, :], X_PS[:, :].rearrange("p (k s) -> p k s", k=KT),
                             ACT.Copy).then_inc(xg_ready, 1)

            def oT_out(cnt, b):
                a.wait_ge(oT_done, cnt)
                a.activation(onehotT[:, b, :, :], O_PS[:, 0:TT * P].rearrange("p (t s) -> p t s", t=TT),
                             ACT.Copy).then_inc(oT_ready, 1)

            def item(it, j, extra):
                i = it * UNROLL
                a.wait_ge(g_clamped, i + (j + 1))
                a.activation(sig, g_lim, ACT.Sigmoid, scale=ALPHA).then_inc(sig_ready, 1)
                xg_out(i + (j + 2 + extra), (j + 1) % 2)
                oT_out(i + (j + 2 + extra), (j + 1) % 2)
                a.wait_ge(aT_done, i + (j + 1))
                a.activation(actT[:, :, :], A_PS[:, :].rearrange("p (q s) -> p q s", q=4),
                             ACT.Copy).then_inc(aT_ready, 1)

            xg_out(1, 0)
            oT_out(1, 0)
            with a.Fori(0, E // UNROLL) as it:
                for j in range(UNROLL):
                    item(it, j, 0)
            a.wait_ge(s_tab, 1)
            more = a.value_load(flag[0:1, 0:1], min_val=0, max_val=1)

            def square_sums(count):
                for t in range(TT):
                    a.wait_ge(acc_done, 2 * count + 2 + t)
                    a.activation(ring[:, t, 0:D], acc[:, t, :], ACT.Square, accum_out=ssq[:, t:t + 1]).then_inc(s_ssq, 1)

            with a.If(more > 0):
                xg_out(E + 2, 0)
                oT_out(E + 2, 0)
                with a.Fori(E // UNROLL, ITEMS // UNROLL) as it:
                    for j in range(UNROLL):
                        item(it, j, 1)
                square_sums(ITEMS)
            with a.Else():
                square_sums(E)
            for t in range(TT):
                a.wait_ge(s_ssq, t + 1)
                a.activation(fin[:, t:t + 1], ssq[:, t:t + 1], ACT.Sqrt, scale=1.0 / D,
                             bias=eps[:, 0:1]).then_inc(s_fr, 1)

        @block.vector
        def _(v):
            n = [0]

            def step(ins):
                n[0] += 1
                ins.then_inc(dve, 1)
                return n[0]

            def link(ins):
                v.wait_ge(dve, step(ins))

            step(v.memset(ones_bf[:, :], 1.0))
            step(v.memset(mean_of[:, :], 1.0 / D))
            step(v.memset(slot[:, :, :], -1.0))
            step(v.memset(gate[:, :, :], 0.0))
            step(v.memset(bsel[:, :], 0.0))
            step(v.memset(upad[:, :, 0:PAD], 0.0))
            v.memset(ysb[:, :], 0.0).then_inc(y_ready, 1)
            for b in range(NB - 1):
                step(v.memset(thr[E * b:E * b + E, :], float(capacity * (b + 1))))
            v.memset(eps[:, :], EPS).then_inc(s_const_v, 1)
            v.wait_ge(dve, n[0])
            v.wait_ge(s_const_v, 1)
            v.wait_ge(s_const, 6)
            for b in range(3):
                step(v.tensor_copy(bsel[E * b:E * b + E, 0:E], ident[0:E, 0:E]))
            v.wait_ge(p_dw, 1)
            v.tensor_copy(dwcol[:, :], bank[1][:, 0:KT * TAPS]).then_inc(v_dw, 1)
            for b in range(2):
                v.wait_ge(p_x, b + 3)
                v.tensor_copy(xT[:, 4 + 2 * b:6 + 2 * b, :],
                              bank[4 + b][:, :].rearrange("p (k s) -> p k s", k=2)).then_inc(v_xv, 1)
            v.wait_ge(s_cact, 1)
            v.tensor_copy(cwide[:, :, :], cact[:, :].unsqueeze(2).to_broadcast([P, KT, 32])).then_inc(s_cwide, 1)

            def rstd_out(k):
                v.wait_ge(s_root, k)
                v.reciprocal(rstd, root).then_inc(s_rstd, 1)
                v.wait_ge(s_rstd, k)

            def over_tiles(ap, k):
                return ap.unsqueeze(1).to_broadcast([P, k, T])

            rstd_out(1)
            v.wait_ge(v_xa, 2)
            v.wait_ge(v_xv, 2)
            link(v.tensor_tensor(hT[:, :, :], xT[:, :, :], over_tiles(rstd, KT), ALU.mult))

            b1f = acc[0:E, :, :].rearrange("p t d -> p (t d)")
            r1 = flat[0:E, :]
            v.wait_ge(s_b1, 16)
            v.tensor_copy(b1s[0:E, :], b1f).then_inc(s_b1f, 1)
            v.wait_ge(s_b1f, 1)
            v.tensor_tensor(r1, b1f, b1s[0:E, :], ALU.subtract).then_inc(s_b1f, 1)
            v.wait_ge(s_b1f, 2)
            v.tensor_copy(b1s[E:2 * E, :], r1).then_inc(s_b1f, 1)
            mid = b1f.bitcast(BF16)[:, 0:2 * F]
            v.tensor_copy(mid, r1).then_inc(s_b1f, 1)
            v.wait_ge(s_b1f, 4)
            v.tensor_tensor(b1s[2 * E:3 * E, :], r1, mid, ALU.subtract).then_inc(s_b1f, 1)

            def modulation(g):
                v.wait_ge(p_row, g + 1)
                turned = bank[0][:, :].rearrange("p (q j r) -> p j q r", q=4, j=4)[:, :, :, 0]
                v.tensor_tensor(modcol[:, g, :].rearrange("p (j q) -> p j q", j=4), turned,
                                vcol[:, AB + 16 * g:AB + 16 * g + 16].rearrange("p (j q) -> p j q", j=4),
                                ALU.add).then_inc(s_mod, 1)
                v.wait_ge(s_mod, g + 1)

            v.wait_ge(v_vec, 1)
            modulation(0)
            link(v.scalar_tensor_tensor(out=a1[:, :], in0=modcol[:, 0, 8:16], scalar=1.0, in1=vcol[:, MG:MG + KT],
                                        op0=ALU.add, op1=ALU.mult))
            for k in range(KT):
                v.tensor_scalar(hT[:, k, :], hT[:, k, :], a1[:, k:k + 1], modcol[:, 0, k:k + 1],
                                ALU.mult, ALU.add).then_inc(s_h, 1)

            def gated(t):
                v.wait_ge(s_glu, t + 1)
                v.scalar_tensor_tensor(out=upad[:, t, PAD:], in0=bank[1 + t % 2][:, 0:T],
                                       scalar=vcol[:, PB1 + t:PB1 + t + 1], in1=glu[:, t % 2, :],
                                       op0=ALU.add, op1=ALU.mult).then_inc(s_u, 1)

            def taps(t):
                sums = [conv[:, t, :], convb]
                last = [0, 0]
                v.wait_ge(s_u, t + 1)
                v.wait_ge(dve, n[0])
                for m in range(PE_TAPS, TAPS):
                    s = m % 2
                    w = dwcol[:, t * TAPS + m:t * TAPS + m + 1]
                    src = upad[:, t, m:m + T]
                    if not last[s]:
                        last[s] = step(v.tensor_scalar(sums[s], src, w, vcol[:, DB + t:DB + t + 1] if s else 0.0,
                                                       ALU.mult, ALU.add))
                    else:
                        v.wait_ge(dve, last[s])
                        last[s] = step(v.scalar_tensor_tensor(out=sums[s], in0=src, scalar=w, in1=sums[s],
                                                              op0=ALU.mult, op1=ALU.add))
                v.wait_ge(dve, n[0])
                link(v.tensor_tensor(sums[0], sums[0], sums[1], ALU.add))
                v.wait_ge(p_taps, t + 1)
                v.tensor_tensor(sums[0], sums[0], bank[3 + t % 2][:, 0:T], ALU.add).then_inc(s_conv, 1)

            for t in range(KT):
                gated(t)
                if t:
                    taps(t - 1)
                if t == 5:
                    modulation(1)
            taps(KT - 1)
            v.wait_ge(p_st, 2)
            v.wait_ge(s_conv, KT)
            for q in range(4):
                v.tensor_tensor(conv[:, 2 * q:2 * q + 2, :], conv[:, 2 * q:2 * q + 2, :],
                                over_tiles(bank[5][:, 0:T], 2), ALU.subtract).then_inc(s_cent, 1)
            modulation(2)
            link(v.tensor_tensor(g1b[:, :], modcol[:, 1, 0:8], vcol[:, PB2:PB2 + KT], ALU.mult))
            link(v.scalar_tensor_tensor(out=a2[:, :], in0=modcol[:, 2, 0:8], scalar=1.0, in1=vcol[:, FG:FG + KT],
                                        op0=ALU.add, op1=ALU.mult))
            v.wait_ge(s_root, 2)
            v.wait_ge(s_cent, 4)
            rstd_out(2)
            for q in range(4):
                v.tensor_tensor(conv[:, 2 * q:2 * q + 2, :], conv[:, 2 * q:2 * q + 2, :],
                                over_tiles(rstd, 2), ALU.mult).then_inc(s_nrm, 1)
            v.wait_ge(p_g2, 1)
            v.wait_ge(s_g2b, 32)
            for r in range(2):
                step(v.tensor_tensor(acc[:, 0, r * H:(r + 1) * H], bank[6 + r][:, :],
                                     acc[:, 0, r * H:(r + 1) * H], ALU.add))
            v.wait_ge(dve, n[0])
            for r in range(2):
                step(v.tensor_copy(g2half[64 * r:64 * r + 64, :], acc[64 * r:64 * r + 64, 0, r * H:(r + 1) * H]))
            for m in range(KT):
                v.wait_ge(s_y2, m + 1)
                v.tensor_tensor(xT[:, m, :], xT[:, m, :], glu[:, m % 2, :], ALU.add).then_inc(s_x2, 1)
            v.wait_ge(s_x2, KT)
            rstd_out(3)
            for q in range(4):
                v.tensor_tensor(hT[:, 2 * q:2 * q + 2, :], xT[:, 2 * q:2 * q + 2, :],
                                over_tiles(rstd, 2), ALU.mult).then_inc(s_n2, 1)
                k = 2 * q + 1
                v.wait_ge(s_n2, q + 1)
                v.tensor_scalar(hT[:, k, :], hT[:, k, :], a2[:, k:k + 1], modcol[:, 1, 8 + k:9 + k],
                                ALU.mult, ALU.add).then_inc(s_h2, 1)
            v.wait_ge(s_n2, 4)
            step(v.memset(onehotT[:, 1, :, :], 0.0))
            v.tensor_tensor(b2g, acc[0:E, 1, :], acc[0:E, 0, :], ALU.mult).then_inc(s_b2g, 1)

            v.wait_ge(p_log, 1)
            v.wait_ge(s_rw, 32)
            v.tensor_scalar(logT[:, :], bank[6][0:E, 0:T], rb[:, 0:1], None, ALU.add).then_inc(s_logT, 1)
            v.wait_ge(p_log2, 1)
            link(v.tensor_copy(logit[:, :, :], bank[7][:, 0:TT * E].rearrange("p (t e) -> p t e", t=TT)))
            for t in range(TT):
                step(v.max(top[:, t, :], logit[:, t, :]))
            v.wait_ge(dve, n[0])
            v.tensor_scalar(negm[:, :], top[:, :, 0], -1.0, None, ALU.mult).then_inc(s_negm, 1)
            for t in range(TT):
                step(v.max_index(topi[:, t, :], top[:, t, :], logit[:, t, :]))
            v.wait_ge(dve, n[0])
            link(v.tensor_copy(topf[:, :, :], topi[:, :, 0:TOP_K]))
            for t in range(TT):
                step(v.tensor_tensor(hits[:, t, :, :], iota_e[:, :].unsqueeze(1).to_broadcast([P, TOP_K, E]),
                                     topf[:, t, :].unsqueeze(2).to_broadcast([P, TOP_K, E]), ALU.is_equal))
            v.wait_ge(dve, n[0])
            link(v.tensor_reduce(mask[:, :, :], hits[:, :, :, :].rearrange("p t k e -> p t e k"), AX.X, ALU.add))
            v.tensor_copy(mask_bf[:, :, :], mask[:, :, :]).then_inc(s_mask, 1)
            v.wait_ge(s_prob, TT)
            link(v.reciprocal(rp4[:, :], psum4[:, :]))
            for t in range(TT):
                step(v.tensor_scalar(gatek[:, t, :], prob[:, t, :], rp4[:, t:t + 1], None, ALU.mult))
            v.wait_ge(dve, n[0])
            for t in range(TT):
                step(v.tensor_tensor(gates4[:, t, :, :], hits[:, t, :, :],
                                     gatek[:, t, :].unsqueeze(2).to_broadcast([P, TOP_K, E]), ALU.mult))
            v.wait_ge(dve, n[0])
            v.tensor_reduce(gate[:, :, 1:E + 1], gates4[:, :, :, :].rearrange("p t k e -> p t e k"), AX.X,
                            ALU.add).then_inc(s_gate, 1)
            v.wait_ge(p_pos, 1)
            link(v.scalar_tensor_tensor(out=slot[:, :, 0:E], in0=bank[0][:, 0:TT * E].rearrange("p (t e) -> p t e", t=TT),
                                        scalar=1.0, in1=mask[:, :, :], op0=ALU.add, op1=ALU.mult))
            link(v.tensor_scalar(slot[:, :, 0:E], slot[:, :, 0:E], -1.0, None, ALU.add))
            link(v.tensor_reduce(most[:, :], bank[0][:, TT * E:TT * E + E], AX.X, ALU.max))
            v.tensor_scalar(flag[:, :], most[:, :], float(capacity), None, ALU.is_gt).then_inc(s_tab, 1)

            def select(i, b, need):
                if need is not None:
                    v.wait_ge(used, need)
                for t in range(TT):
                    v.tensor_scalar(onehot[:, b, t, :], iota_s[:, :, :].rearrange("p a s -> p (a s)"),
                                    slot[:, t, bass.ds(i, 1)], None, ALU.is_equal).then_inc(sel_ready, 1)
                    v.tensor_scalar(onehot_bf[:, b, t, :], iota_s[:, 0, :],
                                    slot[:, t, bass.ds(i, 1)], None, ALU.is_equal).then_inc(sel_ready, 1)
                v.tensor_copy(bias_of[:, b, :], bsel[:, bass.ds(i, 1)].to_broadcast([3 * E, SLOTS])
                              ).then_inc(sel_ready, 1)

            select(0, 0, None)
            v.wait_ge(p_gT, 1)
            v.tensor_copy(gateT[:, :], bank[5][0:E, 0:T]).then_inc(s_gT, 1)

            def take_b2(b):
                t, d0 = b // 2, (b % 2) * 512
                v.wait_ge(p_b2, b + 1)
                v.wait_ge(s_x2c, b + 1)
                ins = v.tensor_tensor(acc[:, t, d0:d0 + 512], acc[:, t, d0:d0 + 512], S_PS[b % 2][:, :], ALU.add)
                ins.then_inc(s_b2r if b < 3 else acc_done, 1)

            for b in range(4):
                t, d0 = b // 2, (b % 2) * 512
                v.wait_ge(s_hi, b + 1)
                if b >= 2:
                    v.wait_ge(s_lo, b - 1)
                v.tensor_tensor(rest[b % 2], bank[1 + b][:, :], hsplit[:, 0, t, d0:d0 + 512], ALU.subtract
                                ).then_inc(s_rest, 1)
                take_b2(b)

            def accumulate(i2, i, t):
                v.wait_ge(sc_done, i2 + t + 1)
                for r in range(2):
                    ins = v.scalar_tensor_tensor(out=acc[:, t, r * H:(r + 1) * H], in0=S_PS[r][:, :],
                                                 scalar=gate[:, t, bass.ds(i, 1)],
                                                 in1=acc[:, t, r * H:(r + 1) * H], op0=ALU.mult, op1=ALU.add)
                ins.then_inc(acc_done, 1)

            def item(it, j):
                i = it * UNROLL
                ch = it * (UNROLL * NCH) + (CH_EXP + NCH * j)
                select(i + (j + 1), (j + 1) % 2, ch - 4)
                v.wait_ge(used, ch + KT)
                v.tensor_scalar(g_lim, G_PS[:, :], LIMIT, None, ALU.min).then_inc(g_clamped, 1)
                v.tensor_scalar(u_lim, U_PS[:, :], LIMIT, -LIMIT, ALU.min, ALU.max).then_inc(u_clamped, 1)
                v.wait_ge(u_clamped, i + (j + 1))
                v.wait_ge(g_clamped, i + (j + 1))
                v.scalar_tensor_tensor(out=u_lim, in0=u_lim, scalar=1.0, in1=g_lim, op0=ALU.add,
                                       op1=ALU.mult).then_inc(mid_act, 1)
                v.wait_ge(mid_act, i + (j + 1))
                v.wait_ge(sig_ready, i + (j + 1))
                v.tensor_tensor(act, u_lim, sig, ALU.mult).then_inc(act_ready, 1)
                for t in range(TT):
                    accumulate(it * (2 * UNROLL) + 2 * j, i + j, t)
                v.wait_ge(used, ch + NCH)
                v.tensor_tensor(ysb[:, :], Y_PS[:, :], g2half[:, :], ALU.mult).then_inc(y_ready, 1)

            v.wait_ge(dve, n[0])
            v.wait_ge(acc_done, 1)
            with v.Fori(0, E // UNROLL) as it:
                for j in range(UNROLL):
                    item(it, j)
            v.wait_ge(s_tab, 1)
            more = v.value_load(flag[0:1, 0:1], min_val=0, max_val=1)

            def last(count):
                for t in range(TT):
                    accumulate(2 * count, count, t)

            with v.If(more > 0):
                k = [0]

                def xlink(ins):
                    k[0] += 1
                    ins.then_inc(x_v, 1)
                    v.wait_ge(x_v, k[0])

                v.wait_ge(xg_ready, E + 1)
                v.wait_ge(oT_ready, E + 1)
                xlink(v.tensor_copy(m3[:, :, :].rearrange("p t (b e) -> p t b e", e=E),
                                    mask_bf[:, :, :].unsqueeze(2).to_broadcast([P, TT, NB - 1, E])))
                v.wait_ge(x_p, 1)
                xlink(v.tensor_tensor(filled[:, :], X_PS[0:CAND, 0:1], thr[:, :], ALU.is_gt))
                xlink(v.tensor_copy(filled_bf[:, :], filled[:, :]))
                v.wait_ge(x_p, 2)
                xlink(v.tensor_copy(rank[:, :], X_PS[0:CAND, 0:1]))
                xlink(v.tensor_scalar(take[:, :], iota_e[0:CAND, 0:EXTRA], rank[:, 0:1], filled[:, 0:1],
                                      ALU.is_equal, ALU.mult))
                xlink(v.tensor_copy(take_bf[:, :], take[:, :]))
                xlink(v.tensor_copy(rep[:, :, :], bsel[:, 0:E].unsqueeze(1).to_broadcast([CAND, 3, E])))
                xlink(v.tensor_tensor(ecol, bsel[:, 0:E], iota_e[0:CAND, :], ALU.mult))
                xlink(v.tensor_reduce(enum[:, :], ecol, AX.X, ALU.add))
                v.wait_ge(x_p, 3)
                xlink(v.tensor_copy(bsel[:, E:E + EXTRA], X_PS[0:CAND, 0:EXTRA]))
                v.wait_ge(x_p, 4)
                v.tensor_copy(eidx, O_PS[0:1, 0:EXTRA]).then_inc(x_sp, 1)
                v.wait_ge(x_sp, 1)
                for b in range(NB - 1):
                    xlink(v.tensor_scalar(t3[:, :, b, :], slot[:, :, 0:E], float(1 - capacity * (b + 1)), None,
                                          ALU.add))
                v.wait_ge(x_p, 5)
                xlink(v.tensor_copy(t3T, O_PS[0:CAND, 0:T]))
                v.wait_ge(x_p, 6)
                xlink(v.tensor_scalar(slot[:, :, E:E + EXTRA],
                                      X_PS[:, 0:TT * EXTRA].rearrange("p (t s) -> p t s", t=TT), -1.0, None,
                                      ALU.add))
                xlink(v.tensor_copy(t3[:, :, :, :], gate[:, :, 1:E + 1].unsqueeze(2)
                                    .to_broadcast([P, TT, NB - 1, E])))
                v.wait_ge(x_p, 7)
                xlink(v.tensor_copy(t3T, O_PS[0:CAND, 0:T]))
                v.wait_ge(x_p, 8)
                xlink(v.tensor_copy(gate[:, :, E + 1:E + 1 + EXTRA],
                                    X_PS[:, 0:TT * EXTRA].rearrange("p (t s) -> p t s", t=TT)))
                select(E, 0, CH_EXP + E * NCH - 4)
                with v.Fori(E // UNROLL, ITEMS // UNROLL) as it:
                    for j in range(UNROLL):
                        item(it, j)
                last(ITEMS)
            with v.Else():
                last(E)
            v.wait_ge(s_fng, 16)
            for t in range(TT):
                v.wait_ge(s_fr, t + 1)
                v.reciprocal(frstd[:, t:t + 1], fin[:, t:t + 1]).then_inc(s_ff, 1)
                v.wait_ge(s_ff, t + 1)
                v.scalar_tensor_tensor(out=acc[:, t, :], in0=acc[:, t, :], scalar=frstd[:, t:t + 1], in1=fng,
                                       op0=ALU.mult, op1=ALU.mult).then_inc(s_fin, 1)

        @block.tensor
        def _(pe):
            mm, tr = pe.matmul, pe.transpose
            pe.wait_ge(s_const, 6)
            pe.wait_ge(s_vec, 16 * 9)
            tr(bank[0][:, 0:120], vrow[0:120, :], ident[0:120, 0:120]).then_inc(p_vec, 1)
            pe.wait_ge(s_dw, 16)
            for k in range(KT):
                ins = tr(bank[1][:, k * TAPS:(k + 1) * TAPS], dwrow[:, k * P:(k + 1) * P], ident[0:TAPS, 0:TAPS])
            ins.then_inc(p_dw, 1)
            pe.wait_ge(s_x, 16)
            for k in range(KT):
                for t in range(TT):
                    ins = tr(bank[2 + k // 2][:, (k % 2) * T + t * P:(k % 2) * T + (t + 1) * P],
                             acc[:, t, k * P:(k + 1) * P], ident[:, :])
                if k % 2:
                    ins.then_inc(p_x, 1)

            def mean(b, src, k):
                return mm(bank[b][:, 0:T], mean_of[:, :], src[:, k, :], start=(k == 0), stop=(k == KT - 1))

            pe.wait_ge(s_const_v, 1)
            for k in range(KT):
                if k % 4 == 0:
                    pe.wait_ge(s_sq, k // 4 + 1)
                ins = mean(6, scratch, k)
            ins.then_inc(p_st, 1)

            def ada(kk):
                g, k = kk // KT, kk % KT
                n = number["ada", kk]
                pe.wait_ge(*chunk_in(n))
                if k == 0 and g:
                    pe.wait_ge(s_row, g)
                for j in range(4):
                    ins = mm(bank[7][32 * j:32 * j + 32, :], cwide[:, k, :], w_slot(n)[:, 512 * j:512 * j + 512],
                             start=(k == 0), stop=(k == KT - 1))
                ins.then_inc(used, 1)

            def turn_row(g):
                pe.wait_ge(s_row, g + 1)
                if g:
                    pe.wait_ge(s_mod, g)
                for q in range(4):
                    ins = tr(bank[0][:, q * P:(q + 1) * P], modrow[:, q * P:(q + 1) * P], ident[:, :])
                ins.then_inc(p_row, 1)

            pe.wait_ge(s_cwide, 1)
            pe.wait_ge(v_vec, 1)
            pe.wait_ge(v_dw, 1)
            for k in range(KT):
                ada(k)
            turn_row(0)

            def taps(t):
                pe.wait_ge(s_u, t + 1)
                pe.wait_ge(s_diag, PE_TAPS * (t + 1))
                if t >= 2:
                    pe.wait_ge(s_conv, t - 1)
                for m in range(PE_TAPS):
                    ins = mm(bank[3 + t % 2][:, 0:T], diag[:, (t % 2) * PE_TAPS + m, :], upad[:, t, m:m + T],
                             start=(m == 0), stop=(m == PE_TAPS - 1))
                ins.then_inc(p_taps, 1)

            for t in range(KT):
                n = number["pw1", t]
                pe.wait_ge(*chunk_in(n))
                w = w_slot(n).rearrange("p (h k n) -> p h k n", h=2, k=KT)
                if t >= 2:
                    pe.wait_ge(s_u, t - 1)
                for h in range(2):
                    for k in range(KT):
                        if t == 0 and h == 0:
                            pe.wait_ge(s_h, k + 1)
                        ins = mm(bank[1 + t % 2][:, h * T:(h + 1) * T], w[:, h, k, :], hT[:, k, :],
                                 start=(k == 0), stop=(k == KT - 1))
                ins.then_inc(used, 1)
                if t:
                    taps(t - 1)
                ada(KT + 2 * t)
                ada(KT + 2 * t + 1)
                if t == 4:
                    turn_row(1)
            taps(KT - 1)
            for k in range(KT):
                pe.wait_ge(s_conv, k + 1)
                ins = mean(5, conv, k)
            ins.then_inc(p_st, 1)
            turn_row(2)
            pe.wait_ge(s_root, 1)
            for k in range(KT):
                pe.wait_ge(s_sq, 2 + k // 2 + 1)
                ins = mean(6, scratch, k)
            ins.then_inc(p_st, 1)
            pe.wait_ge(s_root, 2)
            for r in range(2):
                ins = mm(bank[6 + r][:, :], pick[:, r, :], modrow, start=True, stop=True)
            ins.then_inc(p_g2, 1)
            for m in range(KT):
                n = number["pw2", m // 2]
                if m % 2 == 0:
                    pe.wait_ge(*chunk_in(n))
                w = w_slot(n).rearrange("p (k n) -> p k n", k=KT)
                if m >= 4:
                    pe.wait_ge(s_y2, m - 3)
                for k in range(KT):
                    if m == 0:
                        pe.wait_ge(s_silu, k + 1)
                    ins = mm(bank[1 + m % 4][:, 0:T], w[:, k, (m % 2) * P:(m % 2 + 1) * P], conv[:, k, :],
                             start=(k == 0), stop=(k == KT - 1))
                ins.then_inc(used if m % 2 else p_pw2, 1)
            pe.wait_ge(s_cent, 4)
            for k in range(KT):
                pe.wait_ge(s_sq, 6 + k + 1)
                ins = mean(5, scratch, k)
            ins.then_inc(p_st, 1)
            for b in range(4):
                t, d0 = b // 2, (b % 2) * 4
                for k in range(4):
                    ins = tr(bank[1 + b][:, k * P:(k + 1) * P], xT[:, d0 + k, t * P:(t + 1) * P], ident[:, :])
                ins.then_inc(p_x2, 1)
            pe.wait_ge(s_rw, 32)
            pe.wait_ge(s_h2, KT)
            for k in range(KT):
                ins = mm(bank[6][0:E, 0:T], rw[:, k, :], hT[:, k, :], start=(k == 0), stop=(k == KT - 1))
            ins.then_inc(p_log, 1)
            pe.wait_ge(s_logT, 1)
            for t in range(TT):
                ins = tr(bank[7][:, t * E:(t + 1) * E], logT[:, t * P:(t + 1) * P], ident[0:E, 0:E])
            ins.then_inc(p_log2, 1)
            for b in range(4):
                t, d0 = b // 2, (b % 2) * 4
                pe.wait_ge(s_x2c, b + 1)
                for k in range(4):
                    ins = tr(bank[1 + b][:, k * P:(k + 1) * P], hT[:, d0 + k, t * P:(t + 1) * P], ident[:, :])
                ins.then_inc(p_h2, 1)
            pe.wait_ge(s_mask, 1)
            pos = bank[0]
            mm(pos[:, 0:E], before[:, :], mask_bf[:, 0, :], start=True, stop=True)
            mm(pos[:, E:2 * E], ones_bf[:, :], mask_bf[:, 0, :], start=True, stop=False)
            mm(pos[:, E:2 * E], before[:, :], mask_bf[:, 1, :], start=False, stop=True)
            mm(pos[:, 2 * E:3 * E], ones_bf[:, :], mask_bf[:, 0, :], start=True, stop=False)
            mm(pos[:, 2 * E:3 * E], ones_bf[:, :], mask_bf[:, 1, :], start=False, stop=True).then_inc(p_pos, 1)
            pe.wait_ge(s_gate, 1)
            for t in range(TT):
                ins = tr(bank[5][0:E, t * P:(t + 1) * P], gate[:, t, 1:E + 1], ident[:, :])
            ins.then_inc(p_gT, 1)
            pe.wait_ge(s_gT, 1)
            pe.wait_ge(s_b2g, 1)
            for b in range(4):
                t, d0 = b // 2, (b % 2) * 512
                if b >= 2:
                    pe.wait_ge(s_b2r, b - 1)
                mm(S_PS[b % 2][:, :], gateT[:, t * P:(t + 1) * P], b2g[:, d0:d0 + 512],
                   start=True, stop=True).then_inc(p_b2, 1)

            def turn_onehot(b):
                for t in range(TT):
                    ins = tr(O_PS[:, t * P:(t + 1) * P], onehot[:, b, t, :], ident[:, :])
                ins.then_inc(oT_done, 1)

            def gather(b, selected):
                pe.wait_ge(sel_ready, selected)
                for k in range(KT):
                    for part in range(3):
                        for t in range(TT):
                            ins = mm(X_PS[:, k * SLOTS:(k + 1) * SLOTS], hsplit[:, part, t, k * P:(k + 1) * P],
                                     onehot_bf[:, b, t, :], start=(part == 0 and t == 0),
                                     stop=(part == 2 and t == TT - 1))
                ins.then_inc(xg_done, 1)

            def scatter(b, t):
                for r in range(2):
                    ins = mm(S_PS[r][:, :], onehotT[64 * r:64 * r + 64, b, t, :], ysb[64 * r:64 * r + 64, :],
                             start=True, stop=True)
                ins.then_inc(sc_done, 1)

            def item(it, j, extra):
                i, b = it * UNROLL, j % 2

                def arrived(q):
                    n = CH_EXP + j * NCH + q
                    pe.wait_ge(landed[n % RING], it * (16 * UNROLL * NCH // RING) + 16 * (n // RING + 1))
                    return w_slot(n)

                pe.wait_ge(xg_ready, i + (j + 1 + extra))
                for bk, c0 in ((G_PS, 0), (U_PS, F)):
                    for h in range(2):
                        mm(bk[64 * h:64 * h + 64, :], bias_of[:, b, :], b1s[:, c0 + h * H:c0 + (h + 1) * H],
                           start=True, stop=False)
                for k in range(KT):
                    w = arrived(k)
                    for bk, c0 in ((G_PS, 0), (U_PS, F)):
                        for h in range(2):
                            ins = mm(bk[64 * h:64 * h + 64, :], xg[:, b, k, :], w[:, c0 + h * H:c0 + (h + 1) * H],
                                     start=False, stop=(k == KT - 1))
                    ins.then_inc(used, 1)
                pe.wait_ge(oT_ready, i + (j + 1 + extra))
                pe.wait_ge(y_ready, i + (j + 1))
                pe.wait_ge(acc_done, it * (2 * UNROLL) + (2 * j + 1))
                scatter(1 - b, 0)
                gather(1 - b, it * (5 * UNROLL) + 5 * (j + 2 + extra))
                pe.wait_ge(acc_done, it * (2 * UNROLL) + (2 * j + 2))
                scatter(1 - b, 1)
                turn_onehot(1 - b)
                pe.wait_ge(act_ready, i + (j + 1))
                for q in range(4):
                    ins = tr(A_PS[:, q * P:(q + 1) * P], act[:, q * P:(q + 1) * P], ident[:, :])
                ins.then_inc(aT_done, 1)
                pe.wait_ge(aT_ready, i + (j + 1))
                for q in range(4):
                    w = arrived(KT + q)
                    for f in (2 * q, 2 * q + 1):
                        for r in range(2):
                            ins = mm(Y_PS[64 * r:64 * r + 64, :], actT[:, f % 4, 64 * (f // 4):64 * (f // 4) + 64],
                                     w[:, (f % 2) * D + r * H:(f % 2) * D + (r + 1) * H],
                                     start=(f == 0), stop=(f == 7))
                    ins.then_inc(used, 1)

            def scatter_last(count, extra):
                pe.wait_ge(oT_ready, count + 1 + extra)
                pe.wait_ge(y_ready, count + 1)
                for t in range(TT):
                    pe.wait_ge(acc_done, 2 * count + 1 + t)
                    scatter(1, t)

            pe.wait_ge(sel_ready, 5)
            turn_onehot(0)
            pe.wait_ge(s_lo, 4)
            gather(0, 5)
            with pe.Fori(0, E // UNROLL) as it:
                for j in range(UNROLL):
                    item(it, j, 0)
            pe.wait_ge(s_tab, 1)
            more = pe.value_load(flag[0:1, 0:1], min_val=0, max_val=1)
            with pe.If(more > 0):
                pe.wait_ge(x_v, 1)
                for t in range(TT):
                    ins = mm(X_PS[0:CAND, 0:1], m3[:, t, :], ones_bf[:, 0:1], start=(t == 0), stop=(t == TT - 1))
                ins.then_inc(x_p, 1)
                pe.wait_ge(x_v, 3)
                mm(X_PS[0:CAND, 0:1], before[0:CAND, 0:CAND], filled_bf[:, :], start=True, stop=True).then_inc(x_p, 1)
                pe.wait_ge(x_v, 7)
                mm(X_PS[0:CAND, 0:EXTRA], rep[:, :, :].rearrange("p b e -> p (b e)"), take_bf[:, :],
                   start=True, stop=True).then_inc(x_p, 1)
                pe.wait_ge(x_v, 9)
                mm(O_PS[0:1, 0:EXTRA], enum[:, :], take[:, :], start=True, stop=True).then_inc(x_p, 1)
                for turned, stored in ((13, 14), (16, 17)):
                    pe.wait_ge(x_v, turned)
                    for t in range(TT):
                        ins = tr(O_PS[0:CAND, t * P:(t + 1) * P], t3[:, t, :, :].rearrange("p b e -> p (b e)"),
                                 ident[:, :])
                    ins.then_inc(x_p, 1)
                    pe.wait_ge(x_v, stored)
                    for t in range(TT):
                        ins = mm(X_PS[:, t * EXTRA:(t + 1) * EXTRA], t3T[:, t * P:(t + 1) * P], take[:, :],
                                 start=True, stop=True)
                    ins.then_inc(x_p, 1)
                pe.wait_ge(x_v, 18)
                pe.wait_ge(sel_ready, 5 * (E + 2))
                turn_onehot(0)
                gather(0, 5 * (E + 2))
                with pe.Fori(E // UNROLL, ITEMS // UNROLL) as it:
                    for j in range(UNROLL):
                        item(it, j, 1)
                scatter_last(ITEMS, 1)
            with pe.Else():
                scatter_last(E, 0)


_INS = ["x", "c", "ada_w", "ada_b", "mix_norm_g", "ffn_norm_g", "conf_pw1_w", "conf_pw1_b", "conf_dw_w",
        "conf_dw_b", "conf_ln_g", "conf_ln_b", "conf_pw2_w", "conf_pw2_b", "router_w", "router_b",
        "exp_w1", "exp_b1", "exp_w2", "exp_b2", "final_norm_g"]


def kernel(**inputs):
    import numpy as np
    import concourse.bacc as bacc
    from concourse.bass_utils import run_bass_kernel_spmd

    nc = bacc.Bacc("TRN2", target_bir_lowering=False, num_devices=1)
    arrays, args = {}, []
    for name in _INS:
        arr = np.ascontiguousarray(inputs[name])
        arrays[f"in_{name}"] = arr
        args.append(nc.dram_tensor(f"in_{name}", arr.shape, mybir.dt.from_np(arr.dtype), kind="ExternalInput").ap())
    out = nc.dram_tensor("out", inputs["x"].shape, F32, kind="ExternalOutput").ap()
    build_trunk(nc, *args, out)
    r = run_bass_kernel_spmd(nc, [arrays], core_ids=[0])
    return r.results[0]["out"]
```

```python
from contextlib import ExitStack

import concourse.bass as bass
from concourse import mybir

F32 = mybir.dt.float32
BF16 = mybir.dt.bfloat16
I32 = mybir.dt.int32
U32 = mybir.dt.uint32
ALU = mybir.AluOpType
ACT = mybir.ActivationFunctionType
AX = mybir.AxisListType

P = 128
EPS = 1e-5
LIMIT = 7.0
ALPHA = 1.702
TOP_K = 4
NARROW = 64
WIDE = 128
RING = 12
UNROLL = 2
PE_TAPS = 6
DIAGS = 2 * PE_TAPS


def build_trunk(nc, x, c, ada_w, ada_b, mix_g, ffn_g, pw1_w, pw1_b, dw_w, dw_b, ln_g, ln_b,
                pw2_w, pw2_b, router_w, router_b, exp_w1, exp_b1, exp_w2, exp_b2, final_g, out):
    T, D = x.shape[1], x.shape[2]
    E = router_w.shape[2]
    F = exp_w2.shape[2]
    TAPS = dw_w.shape[1]
    PAD = TAPS - 1
    KT = D // P
    TT = T // P
    H = F // 2
    EXTRA = 8
    NCH = 12
    GROUPS = 3
    stream = [("ada", k) for k in range(KT)]
    for t in range(KT):
        stream += [("pw1", t), ("ada", KT + 2 * t), ("ada", KT + 2 * t + 1)]
    stream += [("pw2", q) for q in range(4)]
    number = {what: n for n, what in enumerate(stream)}
    CH_EXP = len(stream)
    ITEMS = E + EXTRA
    assert E == 32 and T == 2 * WIDE and D == 1024 and NCH == RING and CH_EXP % RING == 0

    ctx = ExitStack()
    with ctx:
        def sb(name, shape, dt=F32):
            return ctx.enter_context(nc.sbuf_tensor(name, shape, dt))

        def sem(name):
            return ctx.enter_context(nc.semaphore(name))

        ring = sb("ring", [P, RING, 2048])
        xT = sb("xT", [P, KT, T])
        hT = sb("hT", [P, KT, T])
        acc = sb("acc", [P, TT, D])
        arena = sb("arena", [P, KT * (PAD + T) + KT * T])
        upad = arena[:, 0:KT * (PAD + T)].rearrange("p (k s) -> p k s", k=KT)
        conv = arena[:, KT * (PAD + T):].rearrange("p (k s) -> p k s", k=KT)
        hsplit = arena[:, 0:3 * TT * D // 2].bitcast(BF16).rearrange("p (a t d) -> p a t d", a=3, t=TT)
        scratch = sb("scratch", [P, KT, T])
        flat = scratch[:, :, :].rearrange("p k s -> p (k s)")
        diag = flat[:, 0:DIAGS * P].rearrange("p (n c) -> p n c", n=DIAGS)
        convb = flat[:, DIAGS * P:DIAGS * P + T]
        g_lim, u_lim = ([flat[:, (2 * n + h) * H:(2 * n + h + 1) * H] for h in range(2)] for n in range(2))
        b2g = flat[0:E, 0:D]
        rest = [flat[:, (2 + n) * H:(3 + n) * H] for n in range(2)]
        glu = sb("glu", [P, 2, T])
        onehot = sb("onehot", [P, 2, TT, P])
        onehotT = sb("onehotT", [P, 2, TT, P])
        vrow = onehot[:, 0, 0, :]
        root, rstd = (onehotT[:, n, :, :].rearrange("p t c -> p (t c)") for n in range(2))
        vcol = sb("vcol", [P, 120])
        dwcol = sb("dwcol", [P, KT * TAPS])
        xg = sb("xg", [P, 2, KT, WIDE])
        dwrow = xg[:, :, :, :].rearrange("p a k s -> p (a k s)")[0:TAPS, 0:D]
        act = sb("act", [P, F])
        actT = sb("actT", [P, 8, P])
        modrow = actT[:, 0:4, :].rearrange("p q c -> p (q c)")
        ysb = sb("ysb", [P, 2, H])
        cact = sb("cact", [P, KT])
        cwide = sb("cwide", [P, KT, 32])
        modcol = sb("modcol", [P, GROUPS, 16])
        a1 = sb("a1", [P, KT])
        a2 = sb("a2", [P, KT])
        g1b = sb("g1b", [P, KT])
        b1s = sb("b1s", [3 * E, 2 * F], BF16)
        b1f = sb("b1f", [E, 2 * F])[:, :]
        b2f = sb("b2f", [E, D])
        g2half = sb("g2half", [P, H])
        g2full = sb("g2full", [P, D])
        rw = sb("rw", [P, KT, E])
        rb = sb("rb", [E, 1])
        ident = sb("ident", [P, P])
        mean_of = sb("mean_of", [P, P])
        ones_bf = sb("ones_bf", [P, P], BF16)
        before = sb("before", [P, P], BF16)
        pick = sb("pick", [P, 2, P])
        iota_n = sb("iota_n", [P, 2, NARROW])
        iota_w = sb("iota_w", [P, WIDE])
        iota_e = sb("iota_e", [P, E])
        eps = sb("eps", [P, 1])
        logT = sb("logT", [E, T])
        gateT = logT
        logit = sb("logit", [P, TT, E])
        top = sb("top", [P, TT, 8])
        topi = sb("topi", [P, TT, 8], U32)
        topf = sb("topf", [P, TT, TOP_K])
        negm = sb("negm", [P, TT])
        prob = sb("prob", [P, TT, TOP_K])
        psum4 = sb("psum4", [P, TT])
        rp4 = sb("rp4", [P, TT])
        gatek = sb("gatek", [P, TT, TOP_K])
        hits, gates4 = (flat[:, at:at + TT * TOP_K * E].rearrange("p (t k e) -> p t k e", t=TT, k=TOP_K)
                        for at in (D, D + TT * TOP_K * E))
        mask = sb("mask", [P, TT, E])
        mask_bf = sb("mask_bf", [P, TT, E], BF16)
        most = sb("most", [P, 1])
        over = sb("over", [P, E])
        wide = sb("wide", [P, E + 2], I32)
        extras = sb("extras", [P, 1], I32)
        slot = sb("slot", [P, TT, ITEMS + 1])
        gate = sb("gate", [P, TT, ITEMS + 1])
        bsel = sb("bsel", [3 * E, ITEMS + 1], BF16)
        onehot_bf = sb("onehot_bf", [P, 2, TT, WIDE], BF16)
        bias_of = sb("bias_of", [3 * E, 2, WIDE], BF16)
        ssq = sb("ssq", [P, TT])
        fin = sb("fin", [P, TT])
        frstd = sb("frstd", [P, TT])
        filled = sb("filled", [E, 1])
        filled_bf = sb("filled_bf", [E, 1], BF16)
        rank = sb("rank", [E, 1])
        take = sb("take", [E, EXTRA])
        take_bf = sb("take_bf", [E, EXTRA], BF16)
        rep3 = sb("rep3", [E, 3, E], BF16)
        enum = sb("enum", [E, 1])
        picked = sb("picked", [E, E])
        eidx = sb("eidx", [1, EXTRA], I32)
        t2 = sb("t2", [P, TT, E])
        t2T = sb("t2T", [E, T])
        fng = xT[:, 0:4, :].rearrange("p k s -> p (k s)")

        bank = [ctx.enter_context(nc.psum_tensor(f"bank{n}", [P, 512], F32)) for n in range(8)]
        S_PS = [bank[6:8], bank[4:6]]

        s_x, s_vec, s_dw, s_b1 = sem("x_in"), sem("vec_in"), sem("dw_in"), sem("b1_in")
        s_rw, s_g2b, s_fng, s_out = sem("rw_in"), sem("late_in"), sem("fng_in"), sem("out_done")
        landed = [sem(f"landed{n}") for n in range(RING)]
        used = sem("chunks_used")
        s_const, s_const_v = sem("const_ready"), sem("const_v_ready")
        p_vec, p_dw, p_x, v_vec, v_dw = sem("vec_turned"), sem("dw_turned"), sem("x_turned"), sem("vcol_ready"), sem("dwcol_ready")
        v_xa, v_xv, s_sq, p_st, s_root, s_rstd = (sem(n) for n in
            ("xT_by_act", "xT_by_dve", "squares_ready", "stat_ready", "root_ready", "rstd_ready"))
        s_cact, s_cwide, s_b1f, s_acc_free = sem("cact_ready"), sem("cwide_ready"), sem("b1_split"), sem("acc_free")
        s_row, p_row, s_mod, s_h = sem("modrow_ready"), sem("modrow_turned"), sem("mod_ready"), sem("h_ready")
        s_glu, s_u, s_diag, p_taps, s_b2r = (sem(n) for n in
            ("glu_ready", "u_ready", "diag_ready", "taps_done", "b2_taken"))
        s_conv, s_cent, s_silu = sem("conv_ready"), sem("centred"), sem("silu_ready")
        s_nrm = sem("ln_normed")
        p_pw2, s_y2, s_x2, s_n2, s_h2 = sem("pw2_done"), sem("y_scaled"), sem("x2_ready"), sem("x2_normed"), sem("h2_ready")
        p_log, s_logT, p_log2, s_logit = sem("logitsT_done"), sem("logT_ready"), sem("logits_done"), sem("logit_ready")
        p_h2, s_hi, s_rest, s_mid, s_lo = sem("h2_turned"), sem("h_hi"), sem("h_rest"), sem("h_mid"), sem("h_lo")
        s_negm, s_prob, s_mask, p_pos, s_tab = sem("negmax_ready"), sem("prob_ready"), sem("mask_ready"), sem("pos_done"), sem("tables_ready")
        s_gate, p_gT, s_gT, p_g2, s_b2g, p_b2, p_x2, s_x2c = (sem(n) for n in
            ("gate_ready", "gate_turned", "gateT_ready", "g2_spread", "b2g_ready", "b2_done", "x2_turned", "x2_copied"))
        dve = sem("vector_steps")
        pool_s = sem("gpsimd_steps")
        sel_ready, xg_done, xg_ready, oT_done, oT_ready = (sem(n) for n in
            ("select_ready", "gathered", "xg_ready", "onehot_turned", "onehotT_ready"))
        g_clamped, sig_ready, act_ready, aT_done, aT_ready = (sem(n) for n in
            ("g_clamped", "sigmoid_ready", "act_ready", "act_turned", "actT_ready"))
        y_ready, sc_done, acc_done, u_clamped, mid_act = (sem(n) for n in
            ("y_ready", "scattered", "accumulated", "u_clamped", "glu_product"))
        x_p, x_v, x_sp = sem("extra_pe"), sem("extra_dve"), sem("extra_experts")
        s_sum, s_ssq, s_fr, s_fin, s_ff = sem("sum_ready"), sem("sumsq_ready"), sem("final_root"), sem("final_scaled"), sem("final_rstd")

        block = ctx.enter_context(nc.Block())

        C0, MG, FG, PB1, DB, LG, LB, PB2, AB = 0, 8, 16, 24, 40, 48, 56, 64, 72

        def w_slot(n):
            return ring[:, n % RING, :]

        def chunk_in(n):
            return landed[n % RING], 16 * (n // RING + 1)

        def widths(eng, it):
            return [eng.value_load(wide[0:1, bass.ds(it * UNROLL + j, 1)], min_val=0, max_val=1)
                    for j in range(UNROLL + 2)]

        def either(eng, is_wide, emit):
            with eng.If(is_wide > 0):
                emit(True)
            with eng.Else():
                emit(False)

        @block.sync
        def _(sp):
            def row(v, at, k):
                sp.dma_start(vrow[at:at + k, :], v.rearrange("(r b) -> r b", b=P)).then_inc(s_vec, 16)

            sp.dma_start(acc[:, :, :], x[0].rearrange("(t p) d -> p t d", p=P)).then_inc(s_x, 16)
            row(c[0], C0, 8)
            row(mix_g[0], MG, 8)
            row(ffn_g[0], FG, 8)
            row(pw1_b[0], PB1, 16)
            row(dw_b[0], DB, 8)
            row(ln_g[0], LG, 8)
            row(ln_b[0], LB, 8)
            row(pw2_b[0], PB2, 8)
            row(ada_b[0], AB, 48)
            sp.dma_start(dwrow, dw_w[0]).then_inc(s_dw, 16)
            sp.dma_start(rw[:, :, :], router_w[0].rearrange("(k p) e -> p k e", p=P)).then_inc(s_rw, 16)
            sp.dma_start(b1f, exp_b1[0]).then_inc(s_b1, 16)
            sp.dma_start(rb[:, :], router_b[0].rearrange("(e a) -> e a", a=1)).then_inc(s_rw, 16)

            pw1_v = pw1_w[0].rearrange("(k p) (h n) -> p h k n", p=P, h=2)
            pw2_v = pw2_w[0].rearrange("(k p) n -> p k n", p=P)
            for n, (what, k) in enumerate(stream):
                if n >= RING:
                    sp.wait_ge(used, n - RING + 1)
                dst = w_slot(n)
                if what == "ada":
                    src = ada_w[0, (k % KT) * P:(k % KT + 1) * P, k // KT * 2048:(k // KT + 1) * 2048]
                elif what == "pw1":
                    dst = dst.rearrange("p (h k n) -> p h k n", h=2, k=KT)
                    src = pw1_v[:, :, :, k * P:(k + 1) * P]
                else:
                    dst = dst.rearrange("p (k n) -> p k n", k=KT)
                    src = pw2_v[:, :, k * 256:(k + 1) * 256]
                sp.dma_start(dst, src).then_inc(landed[n % RING], 16)
                if n == RING - 1:
                    sp.dma_start(g2full[:, :], ada_b[0, 5 * D:6 * D].partition_broadcast(P)).then_inc(s_g2b, 16)
                    sp.dma_start(b2f[:, :], exp_b2[0]).then_inc(s_g2b, 16)

            w1_rows = exp_w1[0].rearrange("e (k p) n -> e k p n", p=P)
            w2_rows = exp_w2[0].rearrange("e (q a p) n -> e q p a n", p=P, a=2)

            def expert(i, e):
                for q in range(NCH):
                    sp.wait_ge(used, i * NCH + (CH_EXP + q - RING + 1))
                    if q < KT:
                        dst = w_slot(q)
                        src = w1_rows[bass.ds(e, 1), q, :, :].rearrange("e p n -> (e p) n")
                    else:
                        dst = w_slot(q).rearrange("p (a n) -> p a n", a=2)
                        src = w2_rows[bass.ds(e, 1), q - KT, :, :, :].rearrange("e p a n -> (e p) a n")
                    sp.dma_start(dst, src).then_inc(landed[q], 16)

            with sp.Fori(0, E) as e:
                expert(e, e)
            sp.wait_ge(s_tab, 1)
            more = sp.value_load(extras[0:1, 0:1], min_val=0, max_val=EXTRA)
            with sp.If(more > 0):
                sp.wait_ge(x_sp, 1)
                with sp.Fori(0, more) as i:
                    e = sp.value_load(eidx[0:1, bass.ds(i, 1)], min_val=0, max_val=E - 1)
                    expert(i + E, e)
            for t in range(TT):
                sp.wait_ge(s_fin, t + 1)
                sp.dma_start(out[0, t * P:(t + 1) * P, :], acc[:, t, :]).then_inc(s_out, 16)
            sp.wait_ge(s_out, 16 * TT)

        @block.gpsimd
        def _(pool):
            n = [0]

            def step(ins):
                n[0] += 1
                ins.then_inc(pool_s, 1)

            step(pool.memset(ident[:, :], 0.0))
            step(pool.memset(pick[:, :, :], 0.0))
            step(pool.memset(before[:, :], 1.0))
            pool.wait_ge(pool_s, 3)
            pool.affine_select(out=ident[:, :], in_=ident[:, :], compare_op=ALU.not_equal, fill=1.0,
                               base=0, pattern=[[-1, P]], channel_multiplier=1).then_inc(s_const, 1)
            for r in range(2):
                pool.affine_select(out=pick[:, r, :], in_=pick[:, r, :], compare_op=ALU.not_equal, fill=1.0,
                                   base=-(64 + 32 * r), pattern=[[0, P]], channel_multiplier=1).then_inc(s_const, 1)
            pool.affine_select(out=before[:, :], in_=before[:, :], compare_op=ALU.is_gt, fill=0.0,
                               base=0, pattern=[[1, P]], channel_multiplier=-1).then_inc(s_const, 1)
            pool.iota(iota_w[:, :], pattern=[[1, WIDE]], base=0, channel_multiplier=0,
                      allow_small_or_imprecise_dtypes=True).then_inc(s_const, 1)
            pool.iota(iota_n[:, :, :], pattern=[[0, 2], [1, NARROW]], base=0, channel_multiplier=0,
                      allow_small_or_imprecise_dtypes=True).then_inc(s_const, 1)
            pool.iota(iota_e[:, :], pattern=[[1, E]], base=0, channel_multiplier=0,
                      allow_small_or_imprecise_dtypes=True).then_inc(s_const, 1)

            for b in range(4):
                t, d0 = b // 2, (b % 2) * 512
                pool.wait_ge(s_mid, b + 1)
                pool.tensor_tensor(hsplit[:, 2, t, d0:d0 + 512], rest[b % 2], hsplit[:, 1, t, d0:d0 + 512],
                                   ALU.subtract).then_inc(s_lo, 1)

        @block.scalar
        def _(a):
            n = [0]

            def step(ins):
                n[0] += 1
                ins.then_inc(act_s, 1)
                return n[0]

            a.wait_ge(p_vec, 1)
            a.activation(vcol[:, :], bank[0][:, 0:120], ACT.Copy).then_inc(v_vec, 1)
            a.wait_ge(v_vec, 1)
            a.activation(cact[:, :], vcol[:, C0:C0 + KT], ACT.Silu).then_inc(s_cact, 1)
            for b in range(2):
                a.wait_ge(p_x, b + 1)
                a.activation(xT[:, 2 * b:2 * b + 2, :], bank[2 + b][:, :].rearrange("p (k s) -> p k s", k=2),
                             ACT.Copy).then_inc(v_xa, 1)

            def squares(lo, hi, src):
                return a.activation(scratch[:, lo:hi, :], src[:, lo:hi, :], ACT.Square)

            a.wait_ge(v_xa, 2)
            squares(0, 4, xT).then_inc(s_sq, 1)
            a.wait_ge(v_xv, 2)
            squares(4, 8, xT).then_inc(s_sq, 1)

            def sqrt(k, b):
                a.wait_ge(p_st, k)
                a.wait_ge(s_const_v, 1)
                a.activation(root, bank[b][:, 0:T], ACT.Sqrt, bias=eps[:, 0:1]).then_inc(s_root, 1)

            sqrt(1, 6)
            def modrow_out(g):
                a.wait_ge(used, number["ada", g * KT + KT - 1] + 1)
                if g:
                    a.wait_ge(p_row, g)
                a.activation(modrow, bank[7][:, :], ACT.Copy).then_inc(s_row, 1)

            modrow_out(0)

            def diagonals(t):
                if t >= 2:
                    a.wait_ge(p_taps, t - 1)
                for m in range(PE_TAPS):
                    s = (t % 2) * PE_TAPS + m
                    a.activation(diag[:, s, :], ident[:, :], ACT.Copy,
                                 scale=dwcol[:, t * TAPS + m:t * TAPS + m + 1]).then_inc(s_diag, 1)

            a.wait_ge(v_dw, 1)
            a.wait_ge(s_b1f, 5)
            diagonals(0)
            for t in range(KT):
                a.wait_ge(used, number["pw1", t] + 1)
                if t >= 2:
                    a.wait_ge(s_u, t - 1)
                a.activation(glu[:, t % 2, :], bank[1 + t % 2][:, T:2 * T], ACT.Sigmoid,
                             bias=vcol[:, PB1 + 8 + t:PB1 + 9 + t]).then_inc(s_glu, 1)
                if t + 1 < KT:
                    diagonals(t + 1)
                if t == 3:
                    modrow_out(1)
            modrow_out(2)

            a.wait_ge(p_taps, KT)
            for q in range(4):
                a.wait_ge(s_cent, q + 1)
                squares(2 * q, 2 * q + 2, conv).then_inc(s_sq, 1)
            sqrt(3, 6)
            for k in range(KT):
                a.wait_ge(s_nrm, k // 2 + 1)
                a.activation(conv[:, k, :], conv[:, k, :], ACT.Silu, scale=vcol[:, LG + k:LG + k + 1],
                             bias=vcol[:, LB + k:LB + k + 1]).then_inc(s_silu, 1)
            for m in range(KT):
                a.wait_ge(p_pw2, m // 2 + 1) if m % 2 == 0 else a.wait_ge(used, number["pw2", m // 2] + 1)
                if m == 0:
                    a.wait_ge(s_mod, 3)
                if m >= 2:
                    a.wait_ge(s_x2, m - 1)
                a.activation(glu[:, m % 2, :], bank[1 + m % 4][:, 0:T], ACT.Identity,
                             scale=modcol[:, 1, m:m + 1], bias=g1b[:, m:m + 1]).then_inc(s_y2, 1)
                if m >= 1:
                    a.wait_ge(s_x2, m)
                    squares(m - 1, m, xT).then_inc(s_sq, 1)
            a.wait_ge(s_x2, KT)
            squares(KT - 1, KT, xT).then_inc(s_sq, 1)
            sqrt(4, 5)
            for k in range(0, KT, 2):
                a.wait_ge(s_n2, k // 2 + 1)
                a.activation(hT[:, k, :], hT[:, k, :], ACT.Identity, scale=a2[:, k:k + 1],
                             bias=modcol[:, 1, 8 + k:9 + k]).then_inc(s_h2, 1)
            for b in range(4):
                t, d0 = b // 2, (b % 2) * 512
                a.wait_ge(p_x2, b + 1)
                a.activation(acc[:, t, d0:d0 + 512], bank[1 + b][:, :], ACT.Copy).then_inc(s_x2c, 1)
            a.dma_start(fng, final_g.partition_broadcast(P)).then_inc(s_fng, 16)
            a.wait_ge(s_negm, 1)
            for t in range(TT):
                a.activation(prob[:, t, :], top[:, t, 0:TOP_K], ACT.Exp, bias=negm[:, t:t + 1],
                             accum_out=psum4[:, t:t + 1]).then_inc(s_prob, 1)
            for b in range(4):
                t, d0 = b // 2, (b % 2) * 512
                a.wait_ge(p_h2, b + 1)
                a.activation(hsplit[:, 0, t, d0:d0 + 512], bank[1 + b][:, :], ACT.Copy).then_inc(s_hi, 1)
                a.wait_ge(s_rest, b + 1)
                a.activation(hsplit[:, 1, t, d0:d0 + 512], rest[b % 2], ACT.Copy).then_inc(s_mid, 1)
            def xg_out(cnt, b, w):
                a.wait_ge(xg_done, cnt)
                if w:
                    a.activation(xg[:, b, 0:4, :], bank[4][:, :].rearrange("p (k s) -> p k s", k=4), ACT.Copy)
                    a.activation(xg[:, b, 4:8, :], bank[5][:, :].rearrange("p (k s) -> p k s", k=4),
                                 ACT.Copy).then_inc(xg_ready, 1)
                else:
                    a.activation(xg[:, b, :, 0:NARROW], bank[4][:, :].rearrange("p (k s) -> p k s", k=KT),
                                 ACT.Copy).then_inc(xg_ready, 1)

            def oT_out(cnt, b):
                a.wait_ge(oT_done, cnt)
                a.activation(onehotT[:, b, :, :], bank[6][:, 0:TT * P].rearrange("p (t s) -> p t s", t=TT),
                             ACT.Copy).then_inc(oT_ready, 1)

            def sigmoids(i2, w):
                c = H if w else H // 2
                for h in range(2):
                    a.wait_ge(g_clamped, i2 + (h + 1))
                    a.activation(act[:, h * c:(h + 1) * c], g_lim[h][:, 0:c], ACT.Sigmoid,
                                 scale=ALPHA).then_inc(sig_ready, 1)

            def actT_out(i2, w):
                q = 4 if w else 2
                for h in range(2):
                    a.wait_ge(aT_done, i2 + (h + 1))
                    a.activation(actT[:, q * h:q * h + q, :],
                                 bank[5 - h][:, 0:q * P].rearrange("p (q s) -> p q s", q=q),
                                 ACT.Copy).then_inc(aT_ready, 1)

            def item(it, j, ws):
                i, i2 = it * UNROLL, it * (2 * UNROLL) + 2 * j
                either(a, ws[j + 1], lambda w: sigmoids(i2, w))
                either(a, ws[j + 2], lambda w: xg_out(i + (j + 2), 1 - j, w))
                oT_out(i + (j + 2), 1 - j)
                either(a, ws[j + 1], lambda w: actT_out(i2, w))

            a.wait_ge(s_tab, 1)
            w0 = a.value_load(wide[0:1, 1:2], min_val=0, max_val=1)
            oT_out(1, 0)
            either(a, w0, lambda w: xg_out(1, 0, w))
            with a.Fori(0, E // UNROLL) as it:
                ws = widths(a, it)
                for j in range(UNROLL):
                    item(it, j, ws)
            more = a.value_load(extras[0:1, 0:1], min_val=0, max_val=EXTRA)
            with a.If(more > 0):
                with a.Fori(0, more) as i:
                    oT_out(i + (E + 2), 0)
                    xg_out(i + (E + 2), 0, True)
                    sigmoids(i * 2 + 2 * E, True)
                    actT_out(i * 2 + 2 * E, True)
            for t in range(TT):
                a.wait_ge(s_sum, 1)
                a.activation(ring[:, t, 0:D], acc[:, t, :], ACT.Square, accum_out=ssq[:, t:t + 1]).then_inc(s_ssq, 1)
            for t in range(TT):
                a.wait_ge(s_ssq, t + 1)
                a.activation(fin[:, t:t + 1], ssq[:, t:t + 1], ACT.Sqrt, scale=1.0 / D,
                             bias=eps[:, 0:1]).then_inc(s_fr, 1)

        @block.vector
        def _(v):
            n = [0]

            def step(ins):
                n[0] += 1
                ins.then_inc(dve, 1)
                return n[0]

            def link(ins):
                v.wait_ge(dve, step(ins))

            step(v.memset(ones_bf[:, :], 1.0))
            step(v.memset(mean_of[:, :], 1.0 / D))
            step(v.memset(slot[:, :, :], -1.0))
            step(v.memset(gate[:, :, :], 0.0))
            step(v.memset(bsel[:, :], 0.0))
            step(v.memset(upad[:, :, 0:PAD], 0.0))
            v.memset(ysb[:, :, :], 0.0).then_inc(y_ready, 1)
            step(v.memset(wide[:, :], 0))
            v.memset(eps[:, :], EPS).then_inc(s_const_v, 1)
            v.wait_ge(dve, n[0])
            v.wait_ge(s_const_v, 1)
            v.wait_ge(s_const, 7)
            for b in range(3):
                step(v.tensor_copy(bsel[E * b:E * b + E, 0:E], ident[0:E, 0:E]))
            v.wait_ge(p_dw, 1)
            v.tensor_copy(dwcol[:, :], bank[1][:, 0:KT * TAPS]).then_inc(v_dw, 1)
            for b in range(2):
                v.wait_ge(p_x, b + 3)
                v.tensor_copy(xT[:, 4 + 2 * b:6 + 2 * b, :],
                              bank[4 + b][:, :].rearrange("p (k s) -> p k s", k=2)).then_inc(v_xv, 1)
            v.wait_ge(s_cact, 1)
            v.tensor_copy(cwide[:, :, :], cact[:, :].unsqueeze(2).to_broadcast([P, KT, 32])).then_inc(s_cwide, 1)

            def rstd_out(k):
                v.wait_ge(s_root, k)
                v.reciprocal(rstd, root).then_inc(s_rstd, 1)
                v.wait_ge(s_rstd, k)

            def over_tiles(ap, k):
                return ap.unsqueeze(1).to_broadcast([P, k, T])

            rstd_out(1)
            v.wait_ge(v_xa, 2)
            v.wait_ge(v_xv, 2)
            link(v.tensor_tensor(hT[:, :, :], xT[:, :, :], over_tiles(rstd, KT), ALU.mult))

            r1 = flat[0:E, :]
            v.wait_ge(s_b1, 16)
            v.tensor_copy(b1s[0:E, :], b1f).then_inc(s_b1f, 1)
            v.wait_ge(s_b1f, 1)
            v.tensor_tensor(r1, b1f, b1s[0:E, :], ALU.subtract).then_inc(s_b1f, 1)
            v.wait_ge(s_b1f, 2)
            v.tensor_copy(b1s[E:2 * E, :], r1).then_inc(s_b1f, 1)
            mid = b1f.bitcast(BF16)[:, 0:2 * F]
            v.tensor_copy(mid, r1).then_inc(s_b1f, 1)
            v.wait_ge(s_b1f, 4)
            v.tensor_tensor(b1s[2 * E:3 * E, :], r1, mid, ALU.subtract).then_inc(s_b1f, 1)

            def modulation(g):
                v.wait_ge(p_row, g + 1)
                turned = bank[0][:, :].rearrange("p (q j r) -> p j q r", q=4, j=4)[:, :, :, 0]
                v.tensor_tensor(modcol[:, g, :].rearrange("p (j q) -> p j q", j=4), turned,
                                vcol[:, AB + 16 * g:AB + 16 * g + 16].rearrange("p (j q) -> p j q", j=4),
                                ALU.add).then_inc(s_mod, 1)
                v.wait_ge(s_mod, g + 1)

            v.wait_ge(v_vec, 1)
            modulation(0)
            link(v.scalar_tensor_tensor(out=a1[:, :], in0=modcol[:, 0, 8:16], scalar=1.0, in1=vcol[:, MG:MG + KT],
                                        op0=ALU.add, op1=ALU.mult))
            for k in range(KT):
                v.tensor_scalar(hT[:, k, :], hT[:, k, :], a1[:, k:k + 1], modcol[:, 0, k:k + 1],
                                ALU.mult, ALU.add).then_inc(s_h, 1)

            def gated(t):
                v.wait_ge(s_glu, t + 1)
                v.scalar_tensor_tensor(out=upad[:, t, PAD:], in0=bank[1 + t % 2][:, 0:T],
                                       scalar=vcol[:, PB1 + t:PB1 + t + 1], in1=glu[:, t % 2, :],
                                       op0=ALU.add, op1=ALU.mult).then_inc(s_u, 1)

            def taps(t):
                sums = [conv[:, t, :], convb]
                last = [0, 0]
                v.wait_ge(s_u, t + 1)
                v.wait_ge(dve, n[0])
                for m in range(PE_TAPS, TAPS):
                    s = m % 2
                    w = dwcol[:, t * TAPS + m:t * TAPS + m + 1]
                    src = upad[:, t, m:m + T]
                    if not last[s]:
                        last[s] = step(v.tensor_scalar(sums[s], src, w, vcol[:, DB + t:DB + t + 1] if s else 0.0,
                                                       ALU.mult, ALU.add))
                    else:
                        v.wait_ge(dve, last[s])
                        last[s] = step(v.scalar_tensor_tensor(out=sums[s], in0=src, scalar=w, in1=sums[s],
                                                              op0=ALU.mult, op1=ALU.add))
                v.wait_ge(dve, n[0])
                link(v.tensor_tensor(sums[0], sums[0], sums[1], ALU.add))
                v.wait_ge(p_taps, t + 1)
                v.tensor_tensor(sums[0], sums[0], bank[3 + t % 2][:, 0:T], ALU.add).then_inc(s_conv, 1)

            for t in range(KT):
                gated(t)
                if t:
                    taps(t - 1)
                if t == 5:
                    modulation(1)
            taps(KT - 1)
            v.wait_ge(p_st, 2)
            v.wait_ge(s_conv, KT)
            for q in range(4):
                v.tensor_tensor(conv[:, 2 * q:2 * q + 2, :], conv[:, 2 * q:2 * q + 2, :],
                                over_tiles(bank[5][:, 0:T], 2), ALU.subtract).then_inc(s_cent, 1)
            modulation(2)
            link(v.tensor_tensor(g1b[:, :], modcol[:, 1, 0:8], vcol[:, PB2:PB2 + KT], ALU.mult))
            link(v.scalar_tensor_tensor(out=a2[:, :], in0=modcol[:, 2, 0:8], scalar=1.0, in1=vcol[:, FG:FG + KT],
                                        op0=ALU.add, op1=ALU.mult))
            v.wait_ge(s_root, 2)
            v.wait_ge(s_cent, 4)
            rstd_out(2)
            for q in range(4):
                v.tensor_tensor(conv[:, 2 * q:2 * q + 2, :], conv[:, 2 * q:2 * q + 2, :],
                                over_tiles(rstd, 2), ALU.mult).then_inc(s_nrm, 1)
            v.wait_ge(p_g2, 1)
            v.wait_ge(s_g2b, 32)
            for r in range(2):
                step(v.tensor_tensor(g2full[:, r * H:(r + 1) * H], bank[6 + r][:, :],
                                     g2full[:, r * H:(r + 1) * H], ALU.add))
            v.wait_ge(dve, n[0])
            for r in range(2):
                step(v.tensor_copy(g2half[64 * r:64 * r + 64, :], g2full[64 * r:64 * r + 64, r * H:(r + 1) * H]))
            for m in range(KT):
                v.wait_ge(s_y2, m + 1)
                v.tensor_tensor(xT[:, m, :], xT[:, m, :], glu[:, m % 2, :], ALU.add).then_inc(s_x2, 1)
            v.wait_ge(s_x2, KT)
            rstd_out(3)
            for q in range(4):
                v.tensor_tensor(hT[:, 2 * q:2 * q + 2, :], xT[:, 2 * q:2 * q + 2, :],
                                over_tiles(rstd, 2), ALU.mult).then_inc(s_n2, 1)
                k = 2 * q + 1
                v.wait_ge(s_n2, q + 1)
                v.tensor_scalar(hT[:, k, :], hT[:, k, :], a2[:, k:k + 1], modcol[:, 1, 8 + k:9 + k],
                                ALU.mult, ALU.add).then_inc(s_h2, 1)
            v.wait_ge(s_n2, 4)
            step(v.memset(onehotT[:, 1, :, :], 0.0))
            v.tensor_tensor(b2g, b2f[:, :], g2full[0:E, :], ALU.mult).then_inc(s_b2g, 1)

            v.wait_ge(p_log, 1)
            v.wait_ge(s_rw, 32)
            v.tensor_scalar(logT[:, :], bank[6][0:E, 0:T], rb[:, 0:1], None, ALU.add).then_inc(s_logT, 1)
            v.wait_ge(p_log2, 1)
            link(v.tensor_copy(logit[:, :, :], bank[7][:, 0:TT * E].rearrange("p (t e) -> p t e", t=TT)))
            for t in range(TT):
                step(v.max(top[:, t, :], logit[:, t, :]))
            v.wait_ge(dve, n[0])
            v.tensor_scalar(negm[:, :], top[:, :, 0], -1.0, None, ALU.mult).then_inc(s_negm, 1)
            for t in range(TT):
                step(v.max_index(topi[:, t, :], top[:, t, :], logit[:, t, :]))
            v.wait_ge(dve, n[0])
            link(v.tensor_copy(topf[:, :, :], topi[:, :, 0:TOP_K]))
            for t in range(TT):
                step(v.tensor_tensor(hits[:, t, :, :], iota_e[:, :].unsqueeze(1).to_broadcast([P, TOP_K, E]),
                                     topf[:, t, :].unsqueeze(2).to_broadcast([P, TOP_K, E]), ALU.is_equal))
            v.wait_ge(dve, n[0])
            link(v.tensor_reduce(mask[:, :, :], hits[:, :, :, :].rearrange("p t k e -> p t e k"), AX.X, ALU.add))
            v.tensor_copy(mask_bf[:, :, :], mask[:, :, :]).then_inc(s_mask, 1)
            v.wait_ge(s_prob, TT)
            link(v.reciprocal(rp4[:, :], psum4[:, :]))
            for t in range(TT):
                step(v.tensor_scalar(gatek[:, t, :], prob[:, t, :], rp4[:, t:t + 1], None, ALU.mult))
            v.wait_ge(dve, n[0])
            for t in range(TT):
                step(v.tensor_tensor(gates4[:, t, :, :], hits[:, t, :, :],
                                     gatek[:, t, :].unsqueeze(2).to_broadcast([P, TOP_K, E]), ALU.mult))
            v.wait_ge(dve, n[0])
            v.tensor_reduce(gate[:, :, 1:E + 1], gates4[:, :, :, :].rearrange("p t k e -> p t e k"), AX.X,
                            ALU.add).then_inc(s_gate, 1)
            v.wait_ge(p_pos, 1)
            link(v.scalar_tensor_tensor(out=slot[:, :, 0:E], in0=bank[0][:, 0:TT * E].rearrange("p (t e) -> p t e", t=TT),
                                        scalar=1.0, in1=mask[:, :, :], op0=ALU.add, op1=ALU.mult))
            link(v.tensor_scalar(slot[:, :, 0:E], slot[:, :, 0:E], -1.0, None, ALU.add))
            counts = bank[0][:, TT * E:TT * E + E]
            step(v.tensor_scalar(wide[:, 1:E + 1], counts, float(NARROW), None, ALU.is_gt))
            link(v.tensor_scalar(over[:, :], counts, float(WIDE), None, ALU.is_gt))
            link(v.tensor_reduce(most[:, :], over[:, :], AX.X, ALU.add))
            v.tensor_copy(extras[:, :], most[:, :]).then_inc(s_tab, 1)
            v.wait_ge(s_tab, 1)

            def select(i, b, w):
                iota = iota_w[:, :] if w else iota_n[:, :, :].rearrange("p a s -> p (a s)")
                m = WIDE if w else NARROW
                for t in range(TT):
                    v.tensor_scalar(onehot[:, b, t, :], iota, slot[:, t, bass.ds(i, 1)], None,
                                    ALU.is_equal).then_inc(sel_ready, 1)
                    v.tensor_scalar(onehot_bf[:, b, t, 0:m], iota[:, 0:m], slot[:, t, bass.ds(i, 1)], None,
                                    ALU.is_equal).then_inc(sel_ready, 1)
                v.tensor_copy(bias_of[:, b, 0:m], bsel[:, bass.ds(i, 1)].to_broadcast([3 * E, m])
                              ).then_inc(sel_ready, 1)

            w0 = v.value_load(wide[0:1, 1:2], min_val=0, max_val=1)
            either(v, w0, lambda w: select(0, 0, w))
            v.wait_ge(p_gT, 1)
            v.tensor_copy(gateT[:, :], bank[5][0:E, 0:T]).then_inc(s_gT, 1)

            def take_b2(b):
                t, d0 = b // 2, (b % 2) * 512
                v.wait_ge(p_b2, b + 1)
                v.wait_ge(s_x2c, b + 1)
                ins = v.tensor_tensor(acc[:, t, d0:d0 + 512], acc[:, t, d0:d0 + 512], bank[6 + b % 2][:, :], ALU.add)
                ins.then_inc(s_b2r if b < 3 else acc_done, 1)

            for b in range(4):
                t, d0 = b // 2, (b % 2) * 512
                v.wait_ge(s_hi, b + 1)
                if b >= 2:
                    v.wait_ge(s_lo, b - 1)
                v.tensor_tensor(rest[b % 2], bank[1 + b][:, :], hsplit[:, 0, t, d0:d0 + 512], ALU.subtract
                                ).then_inc(s_rest, 1)
                take_b2(b)

            def accumulate(i2, i, t):
                v.wait_ge(sc_done, i2 + t + 1)
                for r in range(2):
                    ins = v.scalar_tensor_tensor(out=acc[:, t, r * H:(r + 1) * H], in0=S_PS[t][r][:, :],
                                                 scalar=gate[:, t, bass.ds(i, 1)],
                                                 in1=acc[:, t, r * H:(r + 1) * H], op0=ALU.mult, op1=ALU.add)
                ins.then_inc(acc_done, 1)

            def activations(i2, w):
                c = H if w else H // 2
                for h in range(2):
                    g_ps, u_ps = (bank[2 * h + n][:, :] if w else bank[n][:, h * c:(h + 1) * c] for n in range(2))
                    v.tensor_scalar(g_lim[h][:, 0:c], g_ps, LIMIT, None, ALU.min).then_inc(g_clamped, 1)
                    v.tensor_scalar(u_lim[h][:, 0:c], u_ps, LIMIT, -LIMIT, ALU.min, ALU.max).then_inc(u_clamped, 1)
                for h in range(2):
                    v.wait_ge(u_clamped, i2 + (h + 1))
                    v.wait_ge(g_clamped, i2 + (h + 1))
                    v.scalar_tensor_tensor(out=u_lim[h][:, 0:c], in0=u_lim[h][:, 0:c], scalar=1.0,
                                           in1=g_lim[h][:, 0:c], op0=ALU.add, op1=ALU.mult).then_inc(mid_act, 1)
                for h in range(2):
                    v.wait_ge(mid_act, i2 + (h + 1))
                    v.wait_ge(sig_ready, i2 + (h + 1))
                    v.tensor_tensor(act[:, h * c:(h + 1) * c], act[:, h * c:(h + 1) * c], u_lim[h][:, 0:c],
                                    ALU.mult).then_inc(act_ready, 1)

            def y_out(w):
                if w:
                    v.tensor_tensor(ysb[:, 0, :], bank[2][:, :], g2full[:, 0:H], ALU.mult)
                    v.tensor_tensor(ysb[:, 1, :], bank[3][:, :], g2full[:, H:], ALU.mult).then_inc(y_ready, 1)
                else:
                    v.tensor_tensor(ysb[:, 0, :], bank[2][:, :], g2half[:, :], ALU.mult).then_inc(y_ready, 1)

            def item(it, j, ws):
                i, i2 = it * UNROLL, it * (2 * UNROLL) + 2 * j
                ch = it * (UNROLL * NCH) + (CH_EXP + NCH * j)
                def select_next(w):
                    v.wait_ge(used, ch - 4)
                    select(i + (j + 1), 1 - j, w)

                either(v, ws[j + 2], select_next)
                for t in range(TT):
                    accumulate(i2, i + j, t)

                def middle(w):
                    v.wait_ge(used, ch + KT)
                    activations(i2, w)
                    v.wait_ge(used, ch + NCH)
                    y_out(w)

                either(v, ws[j + 1], middle)

            v.wait_ge(dve, n[0])
            v.wait_ge(acc_done, 1)
            with v.Fori(0, E // UNROLL) as it:
                ws = widths(v, it)
                for j in range(UNROLL):
                    item(it, j, ws)
            for t in range(TT):
                accumulate(2 * E, E, t)
            more = v.value_load(extras[0:1, 0:1], min_val=0, max_val=EXTRA)
            with v.If(more > 0):
                k = [0]

                def xlink(ins):
                    k[0] += 1
                    ins.then_inc(x_v, 1)
                    v.wait_ge(x_v, k[0])

                v.wait_ge(y_ready, E + 1)
                xlink(v.tensor_copy(rep3[:, :, :], ident[0:E, 0:E].unsqueeze(1).to_broadcast([E, 3, E])))
                v.wait_ge(x_p, 1)
                xlink(v.tensor_scalar(filled[:, :], bank[0][0:E, 0:1], float(WIDE), None, ALU.is_gt))
                xlink(v.tensor_copy(filled_bf[:, :], filled[:, :]))
                v.wait_ge(x_p, 2)
                xlink(v.tensor_copy(rank[:, :], bank[1][0:E, 0:1]))
                xlink(v.tensor_scalar(take[:, :], iota_e[0:E, 0:EXTRA], rank[:, 0:1], filled[:, 0:1],
                                      ALU.is_equal, ALU.mult))
                xlink(v.tensor_copy(take_bf[:, :], take[:, :]))
                xlink(v.tensor_tensor(picked[:, :], ident[0:E, 0:E], iota_e[0:E, :], ALU.mult))
                xlink(v.tensor_reduce(enum[:, :], picked[:, :], AX.X, ALU.add))
                v.wait_ge(x_p, 3)
                xlink(v.tensor_copy(bsel[:, E:E + EXTRA], bank[2][0:3 * E, 0:EXTRA]))
                v.wait_ge(x_p, 4)
                v.tensor_copy(eidx[:, :], bank[3][0:1, 0:EXTRA]).then_inc(x_sp, 1)
                v.wait_ge(x_sp, 1)
                xlink(v.tensor_scalar(t2[:, :, :], slot[:, :, 0:E], float(1 - WIDE), None, ALU.add))
                v.wait_ge(x_p, 5)
                xlink(v.tensor_copy(t2T[:, :], bank[0][0:E, 0:T]))
                v.wait_ge(x_p, 6)
                xlink(v.tensor_scalar(slot[:, :, E:E + EXTRA],
                                      bank[1][:, 0:TT * EXTRA].rearrange("p (t s) -> p t s", t=TT), -1.0, None,
                                      ALU.add))
                v.wait_ge(x_p, 7)
                xlink(v.tensor_copy(t2T[:, :], bank[0][0:E, 0:T]))
                v.wait_ge(x_p, 8)
                xlink(v.tensor_copy(gate[:, :, E + 1:E + 1 + EXTRA],
                                    bank[1][:, 0:TT * EXTRA].rearrange("p (t s) -> p t s", t=TT)))
                with v.Fori(0, more) as i:
                    select(i + E, 0, True)
                    v.wait_ge(used, i * NCH + (CH_EXP + E * NCH + KT))
                    activations(i * 2 + 2 * E, True)
                    v.wait_ge(used, i * NCH + (CH_EXP + E * NCH + NCH))
                    y_out(True)
                    for t in range(TT):
                        accumulate(i * 2 + (2 * E + 2), i + (E + 1), t)
                    v.wait_ge(acc_done, i * 2 + (2 * E + 5))
                    v.tensor_copy(most[:, :], eps[:, :]).then_inc(x_v, 1)
                    v.wait_ge(x_v, i + 15)
            with v.Else():
                v.wait_ge(acc_done, 2 * E + 3)
            v.tensor_copy(frstd[:, 0:1], eps[:, :]).then_inc(s_sum, 1)
            v.wait_ge(s_fng, 16)
            for t in range(TT):
                v.wait_ge(s_fr, t + 1)
                v.reciprocal(frstd[:, t:t + 1], fin[:, t:t + 1]).then_inc(s_ff, 1)
                v.wait_ge(s_ff, t + 1)
                v.scalar_tensor_tensor(out=acc[:, t, :], in0=acc[:, t, :], scalar=frstd[:, t:t + 1], in1=fng,
                                       op0=ALU.mult, op1=ALU.mult).then_inc(s_fin, 1)

        @block.tensor
        def _(pe):
            mm, tr = pe.matmul, pe.transpose
            pe.wait_ge(s_const, 7)
            pe.wait_ge(s_vec, 16 * 9)
            tr(bank[0][:, 0:120], vrow[0:120, :], ident[0:120, 0:120]).then_inc(p_vec, 1)
            pe.wait_ge(s_dw, 16)
            for k in range(KT):
                ins = tr(bank[1][:, k * TAPS:(k + 1) * TAPS], dwrow[:, k * P:(k + 1) * P], ident[0:TAPS, 0:TAPS])
            ins.then_inc(p_dw, 1)
            pe.wait_ge(s_x, 16)
            for k in range(KT):
                for t in range(TT):
                    ins = tr(bank[2 + k // 2][:, (k % 2) * T + t * P:(k % 2) * T + (t + 1) * P],
                             acc[:, t, k * P:(k + 1) * P], ident[:, :])
                if k % 2:
                    ins.then_inc(p_x, 1)

            def mean(b, src, k):
                return mm(bank[b][:, 0:T], mean_of[:, :], src[:, k, :], start=(k == 0), stop=(k == KT - 1))

            pe.wait_ge(s_const_v, 1)
            for k in range(KT):
                if k % 4 == 0:
                    pe.wait_ge(s_sq, k // 4 + 1)
                ins = mean(6, scratch, k)
            ins.then_inc(p_st, 1)

            def ada(kk):
                g, k = kk // KT, kk % KT
                n = number["ada", kk]
                pe.wait_ge(*chunk_in(n))
                if k == 0 and g:
                    pe.wait_ge(s_row, g)
                for j in range(4):
                    ins = mm(bank[7][32 * j:32 * j + 32, :], cwide[:, k, :], w_slot(n)[:, 512 * j:512 * j + 512],
                             start=(k == 0), stop=(k == KT - 1))
                ins.then_inc(used, 1)

            def turn_row(g):
                pe.wait_ge(s_row, g + 1)
                if g:
                    pe.wait_ge(s_mod, g)
                for q in range(4):
                    ins = tr(bank[0][:, q * P:(q + 1) * P], modrow[:, q * P:(q + 1) * P], ident[:, :])
                ins.then_inc(p_row, 1)

            pe.wait_ge(s_cwide, 1)
            pe.wait_ge(v_vec, 1)
            pe.wait_ge(v_dw, 1)
            for k in range(KT):
                ada(k)
            turn_row(0)

            def taps(t):
                pe.wait_ge(s_u, t + 1)
                pe.wait_ge(s_diag, PE_TAPS * (t + 1))
                if t >= 2:
                    pe.wait_ge(s_conv, t - 1)
                for m in range(PE_TAPS):
                    ins = mm(bank[3 + t % 2][:, 0:T], diag[:, (t % 2) * PE_TAPS + m, :], upad[:, t, m:m + T],
                             start=(m == 0), stop=(m == PE_TAPS - 1))
                ins.then_inc(p_taps, 1)

            for t in range(KT):
                n = number["pw1", t]
                pe.wait_ge(*chunk_in(n))
                w = w_slot(n).rearrange("p (h k n) -> p h k n", h=2, k=KT)
                if t >= 2:
                    pe.wait_ge(s_u, t - 1)
                for h in range(2):
                    for k in range(KT):
                        if t == 0 and h == 0:
                            pe.wait_ge(s_h, k + 1)
                        ins = mm(bank[1 + t % 2][:, h * T:(h + 1) * T], w[:, h, k, :], hT[:, k, :],
                                 start=(k == 0), stop=(k == KT - 1))
                ins.then_inc(used, 1)
                if t:
                    taps(t - 1)
                ada(KT + 2 * t)
                ada(KT + 2 * t + 1)
                if t == 4:
                    turn_row(1)
            taps(KT - 1)
            for k in range(KT):
                pe.wait_ge(s_conv, k + 1)
                ins = mean(5, conv, k)
            ins.then_inc(p_st, 1)
            turn_row(2)
            pe.wait_ge(s_root, 1)
            for k in range(KT):
                pe.wait_ge(s_sq, 2 + k // 2 + 1)
                ins = mean(6, scratch, k)
            ins.then_inc(p_st, 1)
            pe.wait_ge(s_root, 2)
            for r in range(2):
                ins = mm(bank[6 + r][:, :], pick[:, r, :], modrow, start=True, stop=True)
            ins.then_inc(p_g2, 1)
            for m in range(KT):
                n = number["pw2", m // 2]
                if m % 2 == 0:
                    pe.wait_ge(*chunk_in(n))
                w = w_slot(n).rearrange("p (k n) -> p k n", k=KT)
                if m >= 4:
                    pe.wait_ge(s_y2, m - 3)
                for k in range(KT):
                    if m == 0:
                        pe.wait_ge(s_silu, k + 1)
                    ins = mm(bank[1 + m % 4][:, 0:T], w[:, k, (m % 2) * P:(m % 2 + 1) * P], conv[:, k, :],
                             start=(k == 0), stop=(k == KT - 1))
                ins.then_inc(used if m % 2 else p_pw2, 1)
            pe.wait_ge(s_cent, 4)
            for k in range(KT):
                pe.wait_ge(s_sq, 6 + k + 1)
                ins = mean(5, scratch, k)
            ins.then_inc(p_st, 1)
            for b in range(4):
                t, d0 = b // 2, (b % 2) * 4
                for k in range(4):
                    ins = tr(bank[1 + b][:, k * P:(k + 1) * P], xT[:, d0 + k, t * P:(t + 1) * P], ident[:, :])
                ins.then_inc(p_x2, 1)
            pe.wait_ge(s_rw, 32)
            pe.wait_ge(s_h2, KT)
            for k in range(KT):
                ins = mm(bank[6][0:E, 0:T], rw[:, k, :], hT[:, k, :], start=(k == 0), stop=(k == KT - 1))
            ins.then_inc(p_log, 1)
            pe.wait_ge(s_logT, 1)
            for t in range(TT):
                ins = tr(bank[7][:, t * E:(t + 1) * E], logT[:, t * P:(t + 1) * P], ident[0:E, 0:E])
            ins.then_inc(p_log2, 1)
            for b in range(4):
                t, d0 = b // 2, (b % 2) * 4
                pe.wait_ge(s_x2c, b + 1)
                for k in range(4):
                    ins = tr(bank[1 + b][:, k * P:(k + 1) * P], hT[:, d0 + k, t * P:(t + 1) * P], ident[:, :])
                ins.then_inc(p_h2, 1)
            pe.wait_ge(s_mask, 1)
            pos = bank[0]
            mm(pos[:, 0:E], before[:, :], mask_bf[:, 0, :], start=True, stop=True)
            mm(pos[:, E:2 * E], ones_bf[:, :], mask_bf[:, 0, :], start=True, stop=False)
            mm(pos[:, E:2 * E], before[:, :], mask_bf[:, 1, :], start=False, stop=True)
            mm(pos[:, 2 * E:3 * E], ones_bf[:, :], mask_bf[:, 0, :], start=True, stop=False)
            mm(pos[:, 2 * E:3 * E], ones_bf[:, :], mask_bf[:, 1, :], start=False, stop=True).then_inc(p_pos, 1)
            pe.wait_ge(s_gate, 1)
            for t in range(TT):
                ins = tr(bank[5][0:E, t * P:(t + 1) * P], gate[:, t, 1:E + 1], ident[:, :])
            ins.then_inc(p_gT, 1)
            pe.wait_ge(s_gT, 1)
            pe.wait_ge(s_b2g, 1)
            for b in range(4):
                t, d0 = b // 2, (b % 2) * 512
                if b >= 2:
                    pe.wait_ge(s_b2r, b - 1)
                mm(bank[6 + b % 2][:, :], gateT[:, t * P:(t + 1) * P], b2g[:, d0:d0 + 512],
                   start=True, stop=True).then_inc(p_b2, 1)

            def turn_onehot(b):
                for t in range(TT):
                    ins = tr(bank[6][:, t * P:(t + 1) * P], onehot[:, b, t, :], ident[:, :])
                ins.then_inc(oT_done, 1)

            def gather(b, w):
                m = WIDE if w else NARROW
                per = 512 // m
                for k in range(KT):
                    for part in range(3):
                        for t in range(TT):
                            ins = mm(bank[4 + k // per][:, k % per * m:(k % per + 1) * m],
                                     hsplit[:, part, t, k * P:(k + 1) * P], onehot_bf[:, b, t, 0:m],
                                     start=(part == 0 and t == 0), stop=(part == 2 and t == TT - 1))
                ins.then_inc(xg_done, 1)

            def scatter(b, w):
                for t in range(TT):
                    for r in range(2):
                        if w:
                            ins = mm(S_PS[t][r][:, :], onehotT[:, b, t, :], ysb[:, r, :], start=True, stop=True)
                        else:
                            ins = mm(S_PS[t][r][:, :], onehotT[64 * r:64 * r + 64, b, t, :],
                                     ysb[64 * r:64 * r + 64, 0, :], start=True, stop=True)
                    ins.then_inc(sc_done, 1)

            def arrived(i, q):
                pe.wait_ge(landed[q], i * 16 + 16 * (CH_EXP // RING + 1))
                return w_slot(q)

            def up_bias(b, w):
                for n in range(2):
                    for h in range(2):
                        m, dst = (WIDE, bank[2 * h + n][:, :]) if w else (NARROW, bank[n][64 * h:64 * h + 64, :])
                        mm(dst, bias_of[:, b, 0:m], b1s[:, n * F + h * H:n * F + (h + 1) * H],
                           start=True, stop=False)

            def up(i, b, w, ks):
                for k in ks:
                    wk = arrived(i, k)
                    for n in range(2):
                        for h in range(2):
                            m, dst = (WIDE, bank[2 * h + n][:, :]) if w else (NARROW, bank[n][64 * h:64 * h + 64, :])
                            ins = mm(dst, xg[:, b, k, 0:m], wk[:, n * F + h * H:n * F + (h + 1) * H],
                                     start=False, stop=(k == KT - 1))
                    ins.then_inc(used, 1)

            def down(i, i2, w):
                q = 4 if w else 2
                for h in range(2):
                    pe.wait_ge(act_ready, i2 + (h + 1))
                    for n in range(q):
                        ins = tr(bank[5 - h][:, n * P:(n + 1) * P], act[:, (h * q + n) * P:(h * q + n + 1) * P],
                                 ident[:, :])
                    ins.then_inc(aT_done, 1)
                pe.wait_ge(aT_ready, i2 + 1)
                for f in range(KT):
                    if f == q:
                        pe.wait_ge(aT_ready, i2 + 2)
                    wk = arrived(i, KT + f // 2) if f % 2 == 0 else wk
                    for r in range(2):
                        if w:
                            dst, lhsT = bank[2 + r][:, :], actT[:, f, :]
                        else:
                            dst, lhsT = bank[2][64 * r:64 * r + 64, :], actT[:, f % 4, 64 * (f // 4):64 * (f // 4) + 64]
                        ins = mm(dst, lhsT, wk[:, f % 2 * D + r * H:f % 2 * D + (r + 1) * H],
                                 start=(f == 0), stop=(f == KT - 1))
                    if f % 2:
                        ins.then_inc(used, 1)

            def item(it, j, ws):
                i, i2, b = it * UNROLL, it * (2 * UNROLL) + 2 * j, j
                i = i + j
                pe.wait_ge(xg_ready, i + 1)
                pe.wait_ge(oT_ready, i + 1)

                def first(w):
                    if w:
                        pe.wait_ge(y_ready, i + 1)
                    up_bias(b, w)
                    up(i, b, w, range(2))

                either(pe, ws[j + 1], first)
                pe.wait_ge(y_ready, i + 1)
                pe.wait_ge(acc_done, i2 + 1)
                either(pe, ws[j], lambda w: scatter(1 - b, w))
                either(pe, ws[j + 1], lambda w: up(i, b, w, range(2, KT)))
                pe.wait_ge(sel_ready, i * 5 + 10)
                pe.wait_ge(acc_done, i2 + 3)
                either(pe, ws[j + 2], lambda w: gather(1 - b, w))
                turn_onehot(1 - b)
                pe.wait_ge(xg_ready, i + 2)
                either(pe, ws[j + 1], lambda w: down(i, i2, w))

            pe.wait_ge(s_tab, 1)
            w0 = pe.value_load(wide[0:1, 1:2], min_val=0, max_val=1)
            pe.wait_ge(sel_ready, 5)
            pe.wait_ge(acc_done, 1)
            turn_onehot(0)
            pe.wait_ge(s_lo, 4)
            either(pe, w0, lambda w: gather(0, w))
            with pe.Fori(0, E // UNROLL) as it:
                ws = widths(pe, it)
                for j in range(UNROLL):
                    item(it, j, ws)
            wl = pe.value_load(wide[0:1, E:E + 1], min_val=0, max_val=1)
            pe.wait_ge(y_ready, E + 1)
            pe.wait_ge(oT_ready, E + 1)
            pe.wait_ge(xg_ready, E + 1)
            pe.wait_ge(acc_done, 2 * E + 1)
            either(pe, wl, lambda w: scatter(1, w))
            more = pe.value_load(extras[0:1, 0:1], min_val=0, max_val=EXTRA)
            with pe.If(more > 0):
                pe.wait_ge(x_v, 1)
                for t in range(TT):
                    ins = mm(bank[0][0:E, 0:1], mask_bf[:, t, :], ones_bf[:, 0:1], start=(t == 0), stop=(t == TT - 1))
                ins.then_inc(x_p, 1)
                pe.wait_ge(x_v, 3)
                mm(bank[1][0:E, 0:1], before[0:E, 0:E], filled_bf[:, :], start=True, stop=True).then_inc(x_p, 1)
                pe.wait_ge(x_v, 6)
                mm(bank[2][0:3 * E, 0:EXTRA], rep3[:, :, :].rearrange("p b e -> p (b e)"), take_bf[:, :],
                   start=True, stop=True).then_inc(x_p, 1)
                pe.wait_ge(x_v, 8)
                mm(bank[3][0:1, 0:EXTRA], enum[:, :], take[:, :], start=True, stop=True).then_inc(x_p, 1)
                for turned, src in ((10, t2[:, :, :]), (12, gate[:, :, 1:E + 1])):
                    pe.wait_ge(x_v, turned)
                    for t in range(TT):
                        ins = tr(bank[0][0:E, t * P:(t + 1) * P], src[:, t, :], ident[:, :])
                    ins.then_inc(x_p, 1)
                    pe.wait_ge(x_v, turned + 1)
                    for t in range(TT):
                        ins = mm(bank[1][:, t * EXTRA:(t + 1) * EXTRA], t2T[:, t * P:(t + 1) * P], take[:, :],
                                 start=True, stop=True)
                    ins.then_inc(x_p, 1)
                pe.wait_ge(x_v, 14)
                with pe.Fori(0, more) as i:
                    pe.wait_ge(sel_ready, i * 5 + 5 * (E + 2))
                    pe.wait_ge(acc_done, i * 2 + (2 * E + 3))
                    turn_onehot(0)
                    gather(0, True)
                    pe.wait_ge(xg_ready, i + (E + 2))
                    pe.wait_ge(y_ready, i + (E + 1))
                    up_bias(0, True)
                    up(i + E, 0, True, range(KT))
                    down(i + E, i * 2 + 2 * E, True)
                    pe.wait_ge(y_ready, i + (E + 2))
                    pe.wait_ge(oT_ready, i + (E + 2))
                    scatter(0, True)


_INS = ["x", "c", "ada_w", "ada_b", "mix_norm_g", "ffn_norm_g", "conf_pw1_w", "conf_pw1_b", "conf_dw_w",
        "conf_dw_b", "conf_ln_g", "conf_ln_b", "conf_pw2_w", "conf_pw2_b", "router_w", "router_b",
        "exp_w1", "exp_b1", "exp_w2", "exp_b2", "final_norm_g"]


def kernel(**inputs):
    import numpy as np
    import concourse.bacc as bacc
    from concourse.bass_utils import run_bass_kernel_spmd

    nc = bacc.Bacc("TRN2", target_bir_lowering=False, num_devices=1)
    arrays, args = {}, []
    for name in _INS:
        arr = np.ascontiguousarray(inputs[name])
        arrays[f"in_{name}"] = arr
        args.append(nc.dram_tensor(f"in_{name}", arr.shape, mybir.dt.from_np(arr.dtype), kind="ExternalInput").ap())
    out = nc.dram_tensor("out", inputs["x"].shape, F32, kind="ExternalOutput").ap()
    build_trunk(nc, *args, out)
    r = run_bass_kernel_spmd(nc, [arrays], core_ids=[0])
    return r.results[0]["out"]
```

```python
from contextlib import ExitStack

import concourse.bass as bass
from concourse import mybir

F32 = mybir.dt.float32
BF16 = mybir.dt.bfloat16
I32 = mybir.dt.int32
U32 = mybir.dt.uint32
ALU = mybir.AluOpType
ACT = mybir.ActivationFunctionType
AX = mybir.AxisListType

P = 128
EPS = 1e-5
LIMIT = 7.0
ALPHA = 1.702
TOP_K = 4
NARROW = 64
WIDE = 128
RING = 12
UNROLL = 2
PE_TAPS, PE_TAPS_LAST = 3, 9
POOL_TAPS, POOL_TAPS_LAST = 12, 10
DIAGS = PE_TAPS + PE_TAPS_LAST


def build_trunk(nc, x, c, ada_w, ada_b, mix_g, ffn_g, pw1_w, pw1_b, dw_w, dw_b, ln_g, ln_b,
                pw2_w, pw2_b, router_w, router_b, exp_w1, exp_b1, exp_w2, exp_b2, final_g, out):
    T, D = x.shape[1], x.shape[2]
    E = router_w.shape[2]
    F = exp_w2.shape[2]
    TAPS = dw_w.shape[1]
    PAD = TAPS - 1
    KT = D // P
    TT = T // P
    H = F // 2
    EXTRA = 8
    NCH = 12
    GROUPS = 3
    stream = [("ada", k) for k in range(KT)]
    for t in range(KT):
        stream += [("pw1", t)]
    stream += [("ada", KT + k) for k in range(2 * KT)]
    stream += [("pw2", q) for q in range(4)]
    number = {what: n for n, what in enumerate(stream)}
    CH_EXP = len(stream)
    assert E == 32 and T == 2 * WIDE and D == 1024 and NCH == RING and CH_EXP % RING == 0

    ctx = ExitStack()
    with ctx:
        def sb(name, shape, dt=F32):
            return ctx.enter_context(nc.sbuf_tensor(name, shape, dt))

        def sem(name):
            return ctx.enter_context(nc.semaphore(name))

        def share(t):
            on_pe = PE_TAPS_LAST if t == KT - 1 else PE_TAPS
            return on_pe, on_pe + (POOL_TAPS_LAST if t == KT - 1 else POOL_TAPS)

        diags_to = [sum(share(u)[0] for u in range(t + 1)) for t in range(KT)]

        def pairs(t):
            return (share(t)[1] - share(t)[0]) // 2

        pairs_to = [sum(pairs(u) for u in range(t + 1)) for t in range(KT)]

        ring = sb("ring", [P, RING, 2048])
        xT = sb("xT", [P, KT, T])
        hT = sb("hT", [P, KT, T])
        acc = sb("acc", [P, TT, D])
        arena = sb("arena", [P, KT * (PAD + T) + KT * T])
        upad = arena[:, 0:KT * (PAD + T)].rearrange("p (k s) -> p k s", k=KT)
        conv = arena[:, KT * (PAD + T):].rearrange("p (k s) -> p k s", k=KT)
        hsplit = arena[:, 0:3 * TT * D // 2].bitcast(BF16).rearrange("p (a t d) -> p a t d", a=3, t=TT)
        scratch = sb("scratch", [P, KT, T])
        flat = scratch[:, :, :].rearrange("p k s -> p (k s)")
        diag = flat[:, 0:DIAGS * P].rearrange("p (n c) -> p n c", n=DIAGS)
        convb = flat[:, DIAGS * P:DIAGS * P + T]
        g_lim, u_lim = ([flat[:, (2 * n + h) * H:(2 * n + h + 1) * H] for h in range(2)] for n in range(2))
        b2g = flat[:, 0:H]
        rest = [flat[:, H:2 * H], flat[:, 3 * H:4 * H]] + [
            xT[:, 4 + 2 * n:6 + 2 * n, :].rearrange("p k s -> p (k s)") for n in range(2)]
        glu = sb("glu", [P, 2, T])
        gate4 = glu[:, 0, :].rearrange("p (t r e) -> p t r e", t=TT, r=4)
        gateT4 = glu[:, 1, :]
        onehot = sb("onehot", [P, 2, TT, P])
        onehotT = sb("onehotT", [P, 2, TT, P])
        vrow = onehot[:, 0, 0, :]
        root, rstd = (onehotT[:, n, :, :].rearrange("p t c -> p (t c)") for n in range(2))
        vcol = sb("vcol", [P, 120])
        dwcol = sb("dwcol", [P, KT * TAPS])
        xg = sb("xg", [P, 2, KT, WIDE])
        dwrow = xg[:, :, :, :].rearrange("p a k s -> p (a k s)")[0:TAPS, 0:D]
        act = sb("act", [P, F])
        actT = sb("actT", [P, 8, P])
        poolsum, products = (xg[:, 1 - n, :, :].rearrange("p (b n a) s -> p b n (a s)", b=2, n=2) for n in range(2))

        def pair(n):
            return products[:, n % 2, :, :]

        modrow = actT[:, 0:4, :].rearrange("p q c -> p (q c)")
        ysb = sb("ysb", [P, 2, H])
        cact = sb("cact", [P, KT])
        cwide = sb("cwide", [P, KT, 32])
        modcol = sb("modcol", [P, GROUPS, 16])
        a1 = sb("a1", [P, KT])
        a2 = sb("a2", [P, KT])
        g1b = sb("g1b", [P, KT])
        b1s = sb("b1s", [3 * E, 2 * F], BF16)
        b1f = sb("b1f", [E, 2 * F])[:, :]
        b2f = sb("b2f", [P, H])
        g2half = sb("g2half", [P, H])
        g2full = sb("g2full", [P, D])
        rw = sb("rw", [P, KT, E])
        rb = sb("rb", [E, 1])
        ident = sb("ident", [P, P])
        mean_of = sb("mean_of", [P, P])
        ones_bf = sb("ones_bf", [P, P], BF16)
        before = sb("before", [P, P], BF16)
        pick = sb("pick", [P, 2, P])
        iota_n = sb("iota_n", [P, 2, NARROW])
        iota_w = sb("iota_w", [P, 2, WIDE])
        iota_e = sb("iota_e", [P, E])
        eps = sb("eps", [P, 1])
        logT = sb("logT", [E, T])
        logit = sb("logit", [P, TT, E])
        top = sb("top", [P, TT, 8])
        topi = sb("topi", [P, TT, 8], U32)
        topf = sb("topf", [P, TT, TOP_K])
        negm = sb("negm", [P, TT])
        prob = sb("prob", [P, TT, TOP_K])
        psum4 = sb("psum4", [P, TT])
        rp4 = sb("rp4", [P, TT])
        gatek = sb("gatek", [P, TT, TOP_K])
        hits, gates4 = (flat[:, at:at + TT * TOP_K * E].rearrange("p (t k e) -> p t k e", t=TT, k=TOP_K)
                        for at in (D, D + TT * TOP_K * E))
        mask = sb("mask", [P, TT, E])
        mask_bf = sb("mask_bf", [P, TT, E], BF16)
        most = sb("most", [P, 1])
        over = sb("over", [P, E])
        wide = sb("wide", [P, E + 2], I32)
        extras = sb("extras", [P, 1], I32)
        slot = sb("slot", [P, TT, E + 1])
        gate = sb("gate", [P, TT, E + 1])
        bsel = sb("bsel", [3 * E, E + 1], BF16)
        onehot_bf = sb("onehot_bf", [P, 2, TT, WIDE], BF16)
        bias_of = sb("bias_of", [3 * E, 2, WIDE], BF16)
        ssq = sb("ssq", [P, TT])
        fin = sb("fin", [P, TT])
        frstd = sb("frstd", [P, TT])
        first = sb("first", [P, E])
        order = sb("order", [P, EXTRA])
        eidx = sb("eidx", [1, EXTRA], I32)
        fng = xT[:, 0:4, :].rearrange("p k s -> p (k s)")

        bank = [ctx.enter_context(nc.psum_tensor(f"bank{n}", [P, 512], F32)) for n in range(8)]
        S_PS = [bank[6:8], bank[4:6]]

        s_x, s_vec, s_dw, s_b1 = sem("x_in"), sem("vec_in"), sem("dw_in"), sem("b1_in")
        s_rw, s_g2b, s_fng, s_out = sem("rw_in"), sem("late_in"), sem("fng_in"), sem("out_done")
        landed = [sem(f"landed{n}") for n in range(RING)]
        used = sem("chunks_used")
        s_const, s_const_v = sem("const_ready"), sem("const_v_ready")
        p_vec, p_dw, p_x, v_vec, v_dw = sem("vec_turned"), sem("dw_turned"), sem("x_turned"), sem("vcol_ready"), sem("dwcol_ready")
        v_xa, v_xv, s_sq, p_st, s_root, s_rstd = (sem(n) for n in
            ("xT_by_act", "xT_by_dve", "squares_ready", "stat_ready", "root_ready", "rstd_ready"))
        s_cact, s_cwide, s_b1f = sem("cact_ready"), sem("cwide_ready"), sem("b1_split")
        s_row, p_row, s_mod, s_h = sem("modrow_ready"), sem("modrow_turned"), sem("mod_ready"), sem("h_ready")
        s_glu, s_u, s_diag, p_taps, g_taps, s_prod, g_added = (sem(n) for n in
            ("glu_ready", "u_ready", "diag_ready", "pe_taps_done", "pool_taps_done", "product_ready", "product_added"))
        s_conv, s_cent, s_silu = sem("conv_ready"), sem("centred"), sem("silu_ready")
        s_nrm = sem("ln_normed")
        p_pw2, s_y2, s_x2, s_n2, s_h2 = sem("pw2_done"), sem("y_scaled"), sem("x2_ready"), sem("x2_normed"), sem("h2_ready")
        p_log, s_logT, p_log2 = sem("logitsT_done"), sem("logT_ready"), sem("logits_done")
        p_h2, s_hi, s_rest, s_mid, s_lo = sem("h2_turned"), sem("h_hi"), sem("h_rest"), sem("h_mid"), sem("h_lo")
        s_negm, s_prob, s_mask, p_pos, s_tab = sem("negmax_ready"), sem("prob_ready"), sem("mask_ready"), sem("pos_done"), sem("tables_ready")
        s_h2v, s_lov, s_gate, p_gT, s_gT, p_g2, s_b2g, p_b2, p_x2, s_x2c = (sem(n) for n in
            ("h2_ready_dve", "h_lo_dve", "gate_ready", "gate_turned", "gateT_ready", "g2_spread", "b2g_ready", "b2_done", "x2_turned", "x2_copied"))
        dve = sem("vector_steps")
        pool_s = sem("gpsimd_steps")
        sel_ready, xg_done, xg_ready, oT_done, oT_ready = (sem(n) for n in
            ("select_ready", "gathered", "xg_ready", "onehot_turned", "onehotT_ready"))
        g_clamped, sig_ready, act_ready, aT_done, aT_ready = (sem(n) for n in
            ("g_clamped", "sigmoid_ready", "act_ready", "act_turned", "actT_ready"))
        y_ready, sc_done, acc_done, u_clamped, mid_act = (sem(n) for n in
            ("y_ready", "scattered", "accumulated", "u_clamped", "glu_product"))
        x_sp, x_sel = sem("extra_experts"), sem("extra_selected")
        s_sum, s_ssq, s_fr, s_fin, s_ff = sem("sum_ready"), sem("sumsq_ready"), sem("final_root"), sem("final_scaled"), sem("final_rstd")

        block = ctx.enter_context(nc.Block())

        C0, MG, FG, PB1, DB, LG, LB, PB2, AB = 0, 8, 16, 24, 40, 48, 56, 64, 72

        def w_slot(n):
            return ring[:, n % RING, :]

        def chunk_in(n):
            return landed[n % RING], 16 * (n // RING + 1)

        def widths(eng, it):
            return [eng.value_load(wide[0:1, bass.ds(it * UNROLL + j, 1)], min_val=0, max_val=1)
                    for j in range(UNROLL + 2)]

        def either(eng, is_wide, emit):
            with eng.If(is_wide > 0):
                emit(True)
            with eng.Else():
                emit(False)

        @block.sync
        def _(sp):
            def row(v, at, k):
                sp.dma_start(vrow[at:at + k, :], v.rearrange("(r b) -> r b", b=P)).then_inc(s_vec, 16)

            sp.dma_start(acc[:, :, :], x[0].rearrange("(t p) d -> p t d", p=P)).then_inc(s_x, 16)
            row(c[0], C0, 8)
            row(mix_g[0], MG, 8)
            row(ffn_g[0], FG, 8)
            row(pw1_b[0], PB1, 16)
            row(dw_b[0], DB, 8)
            row(ln_g[0], LG, 8)
            row(ln_b[0], LB, 8)
            row(pw2_b[0], PB2, 8)
            row(ada_b[0], AB, 48)
            sp.dma_start(dwrow, dw_w[0]).then_inc(s_dw, 16)
            sp.dma_start(rw[:, :, :], router_w[0].rearrange("(k p) e -> p k e", p=P)).then_inc(s_rw, 16)
            sp.dma_start(b1f, exp_b1[0]).then_inc(s_b1, 16)
            sp.dma_start(rb[:, :], router_b[0].rearrange("(e a) -> e a", a=1)).then_inc(s_rw, 16)

            pw1_v = pw1_w[0].rearrange("(k p) (h n) -> p h k n", p=P, h=2)
            pw2_v = pw2_w[0].rearrange("(k p) n -> p k n", p=P)
            for n, (what, k) in enumerate(stream):
                if n >= RING:
                    sp.wait_ge(used, n - RING + 1)
                dst = w_slot(n)
                if what == "ada":
                    src = ada_w[0, (k % KT) * P:(k % KT + 1) * P, k // KT * 2048:(k // KT + 1) * 2048]
                elif what == "pw1":
                    dst = dst.rearrange("p (h k n) -> p h k n", h=2, k=KT)
                    src = pw1_v[:, :, :, k * P:(k + 1) * P]
                else:
                    dst = dst.rearrange("p (k n) -> p k n", k=KT)
                    src = pw2_v[:, :, k * 256:(k + 1) * 256]
                sp.dma_start(dst, src).then_inc(landed[n % RING], 16)
                if n == RING - 1:
                    sp.dma_start(g2full[:, :], ada_b[0, 5 * D:6 * D].partition_broadcast(P)).then_inc(s_g2b, 16)
                    for g in range(4):
                        sp.dma_start(b2f[g * E:(g + 1) * E, :],
                                     exp_b2[0, :, g // 2 * H:(g // 2 + 1) * H]).then_inc(s_g2b, 16)

            w1_rows = exp_w1[0].rearrange("e (k p) n -> e k p n", p=P)
            w2_rows = exp_w2[0].rearrange("e (q a p) n -> e q p a n", p=P, a=2)

            def expert(i, e):
                for q in range(NCH):
                    sp.wait_ge(used, i * NCH + (CH_EXP + q - RING + 1))
                    if q < KT:
                        dst = w_slot(q)
                        src = w1_rows[bass.ds(e, 1), q, :, :].rearrange("e p n -> (e p) n")
                    else:
                        dst = w_slot(q).rearrange("p (a n) -> p a n", a=2)
                        src = w2_rows[bass.ds(e, 1), q - KT, :, :, :].rearrange("e p a n -> (e p) a n")
                    sp.dma_start(dst, src).then_inc(landed[q], 16)

            with sp.Fori(0, E) as e:
                expert(e, e)
            sp.wait_ge(s_tab, 1)
            more = sp.value_load(extras[0:1, 0:1], min_val=0, max_val=EXTRA)
            with sp.If(more > 0):
                sp.wait_ge(x_sp, 1)
                with sp.Fori(0, more) as i:
                    e = sp.value_load(eidx[0:1, bass.ds(i, 1)], min_val=0, max_val=E - 1)
                    expert(i + E, e)
            for t in range(TT):
                sp.wait_ge(s_fin, t + 1)
                sp.dma_start(out[0, t * P:(t + 1) * P, :], acc[:, t, :]).then_inc(s_out, 16)
            sp.wait_ge(s_out, 16 * TT)

        @block.gpsimd
        def _(pool):
            n = [0]

            def step(ins):
                n[0] += 1
                ins.then_inc(pool_s, 1)

            added = [0]

            step(pool.memset(ident[:, :], 0.0))
            step(pool.memset(pick[:, :, :], 0.0))
            step(pool.memset(before[:, :], 1.0))
            pool.wait_ge(pool_s, 3)
            pool.affine_select(out=ident[:, :], in_=ident[:, :], compare_op=ALU.not_equal, fill=1.0,
                               base=0, pattern=[[-1, P]], channel_multiplier=1).then_inc(s_const, 1)
            for r in range(2):
                pool.affine_select(out=pick[:, r, :], in_=pick[:, r, :], compare_op=ALU.not_equal, fill=1.0,
                                   base=-(64 + 32 * r), pattern=[[0, P]], channel_multiplier=1).then_inc(s_const, 1)
            pool.affine_select(out=before[:, :], in_=before[:, :], compare_op=ALU.is_gt, fill=0.0,
                               base=0, pattern=[[1, P]], channel_multiplier=-1).then_inc(s_const, 1)
            pool.iota(iota_w[:, :, :], pattern=[[WIDE, 2], [1, WIDE]], base=0, channel_multiplier=0,
                      allow_small_or_imprecise_dtypes=True).then_inc(s_const, 1)
            pool.iota(iota_n[:, :, :], pattern=[[0, 2], [1, NARROW]], base=0, channel_multiplier=0,
                      allow_small_or_imprecise_dtypes=True).then_inc(s_const, 1)
            pool.iota(iota_e[:, :], pattern=[[1, E]], base=0, channel_multiplier=0,
                      allow_small_or_imprecise_dtypes=True).then_inc(s_const, 1)

            for t in range(KT):
                sums = poolsum[:, t % 2, :, :]
                for m in range(1, pairs(t)):
                    pool.wait_ge(s_prod, 2 * (pairs_to[t] - (pairs(t) - 1 - m)))
                    if m > 1:
                        pool.wait_ge(g_added, added[0])
                    pool.tensor_tensor(sums, sums, pair(added[0]), ALU.add).then_inc(g_added, 1)
                    added[0] += 1
                pool.wait_ge(g_added, added[0])
                pool.tensor_tensor(sums[:, 0, :], sums[:, 0, :], sums[:, 1, :], ALU.add).then_inc(g_taps, 1)

            for b in (0, 2):
                t, d0 = b // 2, (b % 2) * 512
                pool.wait_ge(s_mid, b + 1)
                pool.tensor_tensor(hsplit[:, 2, t, d0:d0 + 512], rest[b], hsplit[:, 1, t, d0:d0 + 512],
                                   ALU.subtract).then_inc(s_lo, 1)

        @block.scalar
        def _(a):
            a.wait_ge(p_vec, 1)
            a.activation(vcol[:, :], bank[0][:, 0:120], ACT.Copy).then_inc(v_vec, 1)
            a.wait_ge(v_vec, 1)
            a.activation(cact[:, :], vcol[:, C0:C0 + KT], ACT.Silu).then_inc(s_cact, 1)
            for b in range(2):
                a.wait_ge(p_x, b + 1)
                a.activation(xT[:, 2 * b:2 * b + 2, :], bank[2 + b][:, :].rearrange("p (k s) -> p k s", k=2),
                             ACT.Copy).then_inc(v_xa, 1)

            def squares(lo, hi, src):
                return a.activation(scratch[:, lo:hi, :], src[:, lo:hi, :], ACT.Square)

            a.wait_ge(v_xa, 2)
            squares(0, 4, xT).then_inc(s_sq, 1)
            a.wait_ge(v_xv, 2)
            squares(4, 8, xT).then_inc(s_sq, 1)

            def sqrt(k, b):
                a.wait_ge(p_st, k)
                a.wait_ge(s_const_v, 1)
                a.activation(root, bank[b][:, 0:T], ACT.Sqrt, bias=eps[:, 0:1]).then_inc(s_root, 1)

            sqrt(1, 6)
            def modrow_out(g):
                a.wait_ge(used, number["ada", g * KT + KT - 1] + 1)
                if g:
                    a.wait_ge(p_row, g)
                a.activation(modrow, bank[7][:, :], ACT.Copy).then_inc(s_row, 1)

            modrow_out(0)

            def diagonals(t):
                if t >= 2:
                    a.wait_ge(p_taps, t - 1)
                for m in range(share(t)[0]):
                    s = (t % 2) * PE_TAPS + m
                    a.activation(diag[:, s, :], ident[:, :], ACT.Copy,
                                 scale=dwcol[:, t * TAPS + m:t * TAPS + m + 1]).then_inc(s_diag, 1)

            made = [0]

            def tap_products(t):
                a.wait_ge(s_u, t + 1)
                if t >= 2:
                    a.wait_ge(s_conv, t - 1)
                lo, hi = share(t)
                for m in range(lo, hi, 2):
                    if m == lo:
                        dst = poolsum[:, t % 2, :, :]
                    else:
                        if made[0] >= 2:
                            a.wait_ge(g_added, made[0] - 1)
                        dst = pair(made[0])
                        made[0] += 1
                    for n in range(2):
                        a.activation(dst[:, n, :], upad[:, t, m + n:m + n + T], ACT.Copy,
                                     scale=dwcol[:, t * TAPS + m + n:t * TAPS + m + n + 1]).then_inc(s_prod, 1)

            a.wait_ge(v_dw, 1)
            a.wait_ge(s_b1f, 5)
            diagonals(0)
            for t in range(KT):
                a.wait_ge(used, number["pw1", t] + 1)
                if t >= 2:
                    a.wait_ge(s_u, t - 1)
                a.activation(glu[:, t % 2, :], bank[1 + t % 2][:, T:2 * T], ACT.Sigmoid,
                             bias=vcol[:, PB1 + 8 + t:PB1 + 9 + t]).then_inc(s_glu, 1)
                tap_products(t)
                if t + 1 < KT:
                    diagonals(t + 1)
            modrow_out(1)

            a.wait_ge(p_taps, KT)
            for q in range(4):
                a.wait_ge(s_cent, q + 1)
                squares(2 * q, 2 * q + 2, conv).then_inc(s_sq, 1)
            sqrt(3, 6)
            for k in range(KT):
                a.wait_ge(s_nrm, k // 2 + 1)
                a.activation(conv[:, k, :], conv[:, k, :], ACT.Silu, scale=vcol[:, LG + k:LG + k + 1],
                             bias=vcol[:, LB + k:LB + k + 1]).then_inc(s_silu, 1)
            modrow_out(2)
            for m in range(KT):
                a.wait_ge(p_pw2, m // 2 + 1) if m % 2 == 0 else a.wait_ge(used, number["pw2", m // 2] + 1)
                if m == 0:
                    a.wait_ge(s_mod, 3)
                if m >= 2:
                    a.wait_ge(s_x2, m - 1)
                a.activation(glu[:, m % 2, :], bank[1 + m % 4][:, 0:T], ACT.Identity,
                             scale=modcol[:, 1, m:m + 1], bias=g1b[:, m:m + 1]).then_inc(s_y2, 1)
                if m >= 1:
                    a.wait_ge(s_x2, m)
                    squares(m - 1, m, xT).then_inc(s_sq, 1)
            a.wait_ge(s_x2, KT)
            squares(KT - 1, KT, xT).then_inc(s_sq, 1)
            sqrt(4, 5)
            for k in range(0, KT, 2):
                a.wait_ge(s_n2, k // 2 + 1)
                a.activation(hT[:, k, :], hT[:, k, :], ACT.Identity, scale=a2[:, k:k + 1],
                             bias=modcol[:, 1, 8 + k:9 + k]).then_inc(s_h2, 1)
            for b in range(4):
                t, d0 = b // 2, (b % 2) * 512
                a.wait_ge(p_x2, b + 1)
                a.activation(acc[:, t, d0:d0 + 512], bank[1 + b][:, :], ACT.Copy).then_inc(s_x2c, 1)
            a.dma_start(fng, final_g.partition_broadcast(P)).then_inc(s_fng, 16)
            def high(b):
                t, d0 = b // 2, (b % 2) * 512
                a.wait_ge(p_h2, b + 1)
                a.activation(hsplit[:, 0, t, d0:d0 + 512], bank[1 + b][:, :], ACT.Copy).then_inc(s_hi, 1)

            for b in range(4):
                high(b)
            for b in range(4):
                t, d0 = b // 2, (b % 2) * 512
                a.wait_ge(s_rest, b + 1)
                a.activation(hsplit[:, 1, t, d0:d0 + 512], rest[b], ACT.Copy).then_inc(s_mid, 1)
            a.wait_ge(s_negm, 1)
            for t in range(TT):
                a.activation(prob[:, t, :], top[:, t, 0:TOP_K], ACT.Exp, bias=negm[:, t:t + 1],
                             accum_out=psum4[:, t:t + 1]).then_inc(s_prob, 1)
            def xg_out(cnt, b, w):
                a.wait_ge(xg_done, cnt)
                if w:
                    a.activation(xg[:, b, 0:4, :], bank[4][:, :].rearrange("p (k s) -> p k s", k=4), ACT.Copy)
                    a.activation(xg[:, b, 4:8, :], bank[5][:, :].rearrange("p (k s) -> p k s", k=4),
                                 ACT.Copy).then_inc(xg_ready, 1)
                else:
                    a.activation(xg[:, b, :, 0:NARROW], bank[4][:, :].rearrange("p (k s) -> p k s", k=KT),
                                 ACT.Copy).then_inc(xg_ready, 1)

            def oT_out(cnt, b):
                a.wait_ge(oT_done, cnt)
                a.activation(onehotT[:, b, :, :], bank[6][:, 0:TT * P].rearrange("p (t s) -> p t s", t=TT),
                             ACT.Copy).then_inc(oT_ready, 1)

            def sigmoids(i2, w):
                c = H if w else H // 2
                for h in range(2):
                    a.wait_ge(g_clamped, i2 + (h + 1))
                    a.activation(act[:, h * c:(h + 1) * c], g_lim[h][:, 0:c], ACT.Sigmoid,
                                 scale=ALPHA).then_inc(sig_ready, 1)

            def actT_out(i2, w):
                q = 4 if w else 2
                for h in range(2):
                    a.wait_ge(aT_done, i2 + (h + 1))
                    a.activation(actT[:, q * h:q * h + q, :],
                                 bank[5 - h][:, 0:q * P].rearrange("p (q s) -> p q s", q=q),
                                 ACT.Copy).then_inc(aT_ready, 1)

            def item(it, j, ws):
                i, i2 = it * UNROLL, it * (2 * UNROLL) + 2 * j
                either(a, ws[j + 1], lambda w: sigmoids(i2, w))
                either(a, ws[j + 2], lambda w: xg_out(i + (j + 2), 1 - j, w))
                oT_out(i + (j + 2), 1 - j)
                either(a, ws[j + 1], lambda w: actT_out(i2, w))

            a.wait_ge(s_tab, 1)
            w0 = a.value_load(wide[0:1, 1:2], min_val=0, max_val=1)
            oT_out(1, 0)
            either(a, w0, lambda w: xg_out(1, 0, w))
            with a.Fori(0, E // UNROLL) as it:
                ws = widths(a, it)
                for j in range(UNROLL):
                    item(it, j, ws)
            more = a.value_load(extras[0:1, 0:1], min_val=0, max_val=EXTRA)
            with a.If(more > 0):
                with a.Fori(0, more) as i:
                    with a.If(i > 0):
                        oT_out(i + (E + 1), 0)
                        xg_out(i + (E + 1), 0, True)
                    sigmoids(i * 2 + 2 * E, True)
                    actT_out(i * 2 + 2 * E, True)
            for t in range(TT):
                a.wait_ge(s_sum, 1)
                a.activation(ring[:, t, 0:D], acc[:, t, :], ACT.Square, accum_out=ssq[:, t:t + 1]).then_inc(s_ssq, 1)
            for t in range(TT):
                a.wait_ge(s_ssq, t + 1)
                a.activation(fin[:, t:t + 1], ssq[:, t:t + 1], ACT.Sqrt, scale=1.0 / D,
                             bias=eps[:, 0:1]).then_inc(s_fr, 1)

        @block.vector
        def _(v):
            n = [0]

            def step(ins):
                n[0] += 1
                ins.then_inc(dve, 1)
                return n[0]

            def link(ins):
                v.wait_ge(dve, step(ins))

            step(v.memset(ones_bf[:, :], 1.0))
            step(v.memset(mean_of[:, :], 1.0 / D))
            step(v.memset(slot[:, :, :], -1.0))
            step(v.memset(gate[:, :, :], 0.0))
            step(v.memset(bsel[:, :], 0.0))
            step(v.memset(upad[:, :, 0:PAD], 0.0))
            v.memset(ysb[:, :, :], 0.0).then_inc(y_ready, 1)
            step(v.memset(wide[:, :], 0))
            v.memset(eps[:, :], EPS).then_inc(s_const_v, 1)
            v.wait_ge(dve, n[0])
            v.wait_ge(s_const_v, 1)
            v.wait_ge(s_const, 7)
            for b in range(3):
                step(v.tensor_copy(bsel[E * b:E * b + E, 0:E], ident[0:E, 0:E]))
            v.wait_ge(p_dw, 1)
            v.tensor_copy(dwcol[:, :], bank[1][:, 0:KT * TAPS]).then_inc(v_dw, 1)
            for b in range(2):
                v.wait_ge(p_x, b + 3)
                v.tensor_copy(xT[:, 4 + 2 * b:6 + 2 * b, :],
                              bank[4 + b][:, :].rearrange("p (k s) -> p k s", k=2)).then_inc(v_xv, 1)
            v.wait_ge(s_cact, 1)
            v.tensor_copy(cwide[:, :, :], cact[:, :].unsqueeze(2).to_broadcast([P, KT, 32])).then_inc(s_cwide, 1)

            def rstd_out(k):
                v.wait_ge(s_root, k)
                v.reciprocal(rstd, root).then_inc(s_rstd, 1)
                v.wait_ge(s_rstd, k)

            def over_tiles(ap, k):
                return ap.unsqueeze(1).to_broadcast([P, k, T])

            rstd_out(1)
            v.wait_ge(v_xa, 2)
            v.wait_ge(v_xv, 2)
            link(v.tensor_tensor(hT[:, :, :], xT[:, :, :], over_tiles(rstd, KT), ALU.mult))

            r1 = flat[0:E, :]
            v.wait_ge(s_b1, 16)
            v.tensor_copy(b1s[0:E, :], b1f).then_inc(s_b1f, 1)
            v.wait_ge(s_b1f, 1)
            v.tensor_tensor(r1, b1f, b1s[0:E, :], ALU.subtract).then_inc(s_b1f, 1)
            v.wait_ge(s_b1f, 2)
            v.tensor_copy(b1s[E:2 * E, :], r1).then_inc(s_b1f, 1)
            mid = b1f.bitcast(BF16)[:, 0:2 * F]
            v.tensor_copy(mid, r1).then_inc(s_b1f, 1)
            v.wait_ge(s_b1f, 4)
            v.tensor_tensor(b1s[2 * E:3 * E, :], r1, mid, ALU.subtract).then_inc(s_b1f, 1)

            def modulation(g):
                v.wait_ge(p_row, g + 1)
                turned = bank[0][:, :].rearrange("p (q j r) -> p j q r", q=4, j=4)[:, :, :, 0]
                v.tensor_tensor(modcol[:, g, :].rearrange("p (j q) -> p j q", j=4), turned,
                                vcol[:, AB + 16 * g:AB + 16 * g + 16].rearrange("p (j q) -> p j q", j=4),
                                ALU.add).then_inc(s_mod, 1)
                v.wait_ge(s_mod, g + 1)

            v.wait_ge(v_vec, 1)
            modulation(0)
            link(v.scalar_tensor_tensor(out=a1[:, :], in0=modcol[:, 0, 8:16], scalar=1.0, in1=vcol[:, MG:MG + KT],
                                        op0=ALU.add, op1=ALU.mult))
            for k in range(KT):
                v.tensor_scalar(hT[:, k, :], hT[:, k, :], a1[:, k:k + 1], modcol[:, 0, k:k + 1],
                                ALU.mult, ALU.add).then_inc(s_h, 1)

            def gated(t):
                v.wait_ge(s_glu, t + 1)
                v.scalar_tensor_tensor(out=upad[:, t, PAD:], in0=bank[1 + t % 2][:, 0:T],
                                       scalar=vcol[:, PB1 + t:PB1 + t + 1], in1=glu[:, t % 2, :],
                                       op0=ALU.add, op1=ALU.mult).then_inc(s_u, 1)

            def taps(t):
                sums = [conv[:, t, :], convb]
                last = [0, 0]
                v.wait_ge(s_u, t + 1)
                v.wait_ge(dve, n[0])
                for m in range(share(t)[1], TAPS):
                    s = m % 2
                    w = dwcol[:, t * TAPS + m:t * TAPS + m + 1]
                    src = upad[:, t, m:m + T]
                    if not last[s]:
                        last[s] = step(v.tensor_scalar(sums[s], src, w, vcol[:, DB + t:DB + t + 1] if s else 0.0,
                                                       ALU.mult, ALU.add))
                    else:
                        v.wait_ge(dve, last[s])
                        last[s] = step(v.scalar_tensor_tensor(out=sums[s], in0=src, scalar=w, in1=sums[s],
                                                              op0=ALU.mult, op1=ALU.add))
                    if t and m == share(t)[1] + 5:
                        others_taps(t - 1)
                v.wait_ge(dve, n[0])
                link(v.tensor_tensor(sums[0], sums[0], sums[1], ALU.add))

            def others_taps(t):
                v.wait_ge(p_taps, t + 1)
                link(v.tensor_tensor(conv[:, t, :], conv[:, t, :], bank[3 + t % 2][:, 0:T], ALU.add))
                v.wait_ge(g_taps, t + 1)
                v.tensor_tensor(conv[:, t, :], conv[:, t, :], poolsum[:, t % 2, 0, :], ALU.add).then_inc(s_conv, 1)

            for t in range(KT):
                gated(t)
                taps(t)
            others_taps(KT - 1)
            v.wait_ge(p_st, 2)
            v.wait_ge(s_conv, KT)
            for q in range(4):
                v.tensor_tensor(conv[:, 2 * q:2 * q + 2, :], conv[:, 2 * q:2 * q + 2, :],
                                over_tiles(bank[5][:, 0:T], 2), ALU.subtract).then_inc(s_cent, 1)
            modulation(1)
            link(v.tensor_tensor(g1b[:, :], modcol[:, 1, 0:8], vcol[:, PB2:PB2 + KT], ALU.mult))
            v.wait_ge(s_root, 2)
            v.wait_ge(s_cent, 4)
            rstd_out(2)
            for q in range(4):
                v.tensor_tensor(conv[:, 2 * q:2 * q + 2, :], conv[:, 2 * q:2 * q + 2, :],
                                over_tiles(rstd, 2), ALU.mult).then_inc(s_nrm, 1)
            modulation(2)
            link(v.scalar_tensor_tensor(out=a2[:, :], in0=modcol[:, 2, 0:8], scalar=1.0, in1=vcol[:, FG:FG + KT],
                                        op0=ALU.add, op1=ALU.mult))
            v.wait_ge(p_g2, 1)
            v.wait_ge(s_g2b, 16 * 5)
            for r in range(2):
                step(v.tensor_tensor(g2full[:, r * H:(r + 1) * H], bank[6 + r][:, :],
                                     g2full[:, r * H:(r + 1) * H], ALU.add))
            v.wait_ge(dve, n[0])
            for r in range(2):
                step(v.tensor_copy(g2half[64 * r:64 * r + 64, :], g2full[64 * r:64 * r + 64, r * H:(r + 1) * H]))
            for m in range(KT):
                v.wait_ge(s_y2, m + 1)
                v.tensor_tensor(xT[:, m, :], xT[:, m, :], glu[:, m % 2, :], ALU.add).then_inc(s_x2, 1)
            v.wait_ge(s_x2, KT)
            rstd_out(3)
            for q in range(5):
                if q < 4:
                    v.tensor_tensor(hT[:, 2 * q:2 * q + 2, :], xT[:, 2 * q:2 * q + 2, :],
                                    over_tiles(rstd, 2), ALU.mult).then_inc(s_n2, 1)
                if q:
                    k = 2 * q - 1
                    v.wait_ge(s_n2, q)
                    v.tensor_scalar(hT[:, k, :], hT[:, k, :], a2[:, k:k + 1], modcol[:, 1, 8 + k:9 + k],
                                    ALU.mult, ALU.add).then_inc(s_h2v, 1)
            v.wait_ge(s_n2, 4)
            step(v.memset(onehotT[:, 1, :, :], 0.0))
            v.wait_ge(dve, n[0])
            v.tensor_tensor(b2g, b2f[:, :], g2half[:, :], ALU.mult).then_inc(s_b2g, 1)

            v.wait_ge(p_log, 1)
            v.wait_ge(s_rw, 32)
            v.tensor_scalar(logT[:, :], bank[6][0:E, 0:T], rb[:, 0:1], None, ALU.add).then_inc(s_logT, 1)
            v.wait_ge(p_log2, 1)
            link(v.tensor_copy(logit[:, :, :], bank[7][:, 0:TT * E].rearrange("p (t e) -> p t e", t=TT)))
            for t in range(TT):
                step(v.max(top[:, t, :], logit[:, t, :]))
            v.wait_ge(dve, n[0])
            v.tensor_scalar(negm[:, :], top[:, :, 0], -1.0, None, ALU.mult).then_inc(s_negm, 1)
            for t in range(TT):
                step(v.max_index(topi[:, t, :], top[:, t, :], logit[:, t, :]))
            v.wait_ge(dve, n[0])
            link(v.tensor_copy(topf[:, :, :], topi[:, :, 0:TOP_K]))
            for t in range(TT):
                step(v.tensor_tensor(hits[:, t, :, :], iota_e[:, :].unsqueeze(1).to_broadcast([P, TOP_K, E]),
                                     topf[:, t, :].unsqueeze(2).to_broadcast([P, TOP_K, E]), ALU.is_equal))
            v.wait_ge(dve, n[0])
            link(v.tensor_reduce(mask[:, :, :], hits[:, :, :, :].rearrange("p t k e -> p t e k"), AX.X, ALU.add))
            v.tensor_copy(mask_bf[:, :, :], mask[:, :, :]).then_inc(s_mask, 1)
            def rest_of(b):
                t, d0 = b // 2, (b % 2) * 512
                v.wait_ge(s_hi, b + 1)
                v.tensor_tensor(rest[b], bank[1 + b][:, :], hsplit[:, 0, t, d0:d0 + 512], ALU.subtract
                                ).then_inc(s_rest, 1)

            def low(b):
                t, d0 = b // 2, (b % 2) * 512
                v.wait_ge(s_mid, b + 1)
                v.tensor_tensor(hsplit[:, 2, t, d0:d0 + 512], rest[b], hsplit[:, 1, t, d0:d0 + 512],
                                ALU.subtract).then_inc(s_lov, 1)

            rest_of(0)
            rest_of(1)
            v.wait_ge(p_pos, 1)
            link(v.scalar_tensor_tensor(out=slot[:, :, 0:E], in0=bank[0][:, 0:TT * E].rearrange("p (t e) -> p t e", t=TT),
                                        scalar=1.0, in1=mask[:, :, :], op0=ALU.add, op1=ALU.mult))
            link(v.tensor_scalar(slot[:, :, 0:E], slot[:, :, 0:E], -1.0, None, ALU.add))
            counts = bank[0][:, TT * E:TT * E + E]
            step(v.tensor_scalar(wide[:, 1:E + 1], counts, float(NARROW), None, ALU.is_gt))
            link(v.tensor_scalar(over[:, :], counts, float(WIDE), None, ALU.is_gt))
            link(v.tensor_reduce(most[:, :], over[:, :], AX.X, ALU.add))
            step(v.tensor_scalar(wide[:, E + 1:E + 2], most[:, :], 0.0, None, ALU.is_gt))
            v.tensor_copy(extras[:, :], most[:, :]).then_inc(s_tab, 1)
            rest_of(2)
            rest_of(3)
            v.wait_ge(s_tab, 1)

            def select(i, b, w, second=0):
                iota = iota_w[:, second, :] if w else iota_n[:, :, :].rearrange("p a s -> p (a s)")
                m = WIDE if w else NARROW
                for t in range(TT):
                    v.tensor_scalar(onehot[:, b, t, :], iota, slot[:, t, bass.ds(i, 1)], None,
                                    ALU.is_equal).then_inc(sel_ready, 1)
                    v.tensor_scalar(onehot_bf[:, b, t, 0:m], iota[:, 0:m], slot[:, t, bass.ds(i, 1)], None,
                                    ALU.is_equal).then_inc(sel_ready, 1)
                v.tensor_copy(bias_of[:, b, 0:m], bsel[:, bass.ds(i, 1)].to_broadcast([3 * E, m])
                              ).then_inc(sel_ready, 1)

            w0 = v.value_load(wide[0:1, 1:2], min_val=0, max_val=1)
            either(v, w0, lambda w: select(0, 0, w))
            low(1)
            low(3)
            v.wait_ge(s_prob, TT)
            link(v.reciprocal(rp4[:, :], psum4[:, :]))
            for t in range(TT):
                step(v.tensor_scalar(gatek[:, t, :], prob[:, t, :], rp4[:, t:t + 1], None, ALU.mult))
            v.wait_ge(dve, n[0])
            for t in range(TT):
                step(v.tensor_tensor(gates4[:, t, :, :], hits[:, t, :, :],
                                     gatek[:, t, :].unsqueeze(2).to_broadcast([P, TOP_K, E]), ALU.mult))
            v.wait_ge(dve, n[0])
            link(v.tensor_reduce(gate[:, :, 1:E + 1], gates4[:, :, :, :].rearrange("p t k e -> p t e k"), AX.X,
                                 ALU.add))
            for t in range(TT):
                v.tensor_copy(gate4[:, t, :, :], gate[:, t, 1:E + 1].unsqueeze(1).to_broadcast([P, 4, E])
                              ).then_inc(s_gate, 1)
            v.wait_ge(p_gT, 1)
            v.tensor_copy(gateT4, bank[7][:, 0:T]).then_inc(s_gT, 1)

            def take_b2():
                v.wait_ge(p_b2, 1)
                v.wait_ge(s_x2c, 4)
                for t in range(TT):
                    for r in range(2):
                        ins = v.tensor_tensor(acc[:, t, r * H:(r + 1) * H], acc[:, t, r * H:(r + 1) * H],
                                              S_PS[t][r][:, :], ALU.add)
                ins.then_inc(acc_done, 1)

            def accumulate(i2, i, t):
                v.wait_ge(sc_done, i2 + t + 1)
                for r in range(2):
                    ins = v.scalar_tensor_tensor(out=acc[:, t, r * H:(r + 1) * H], in0=S_PS[t][r][:, :],
                                                 scalar=gate[:, t, bass.ds(i, 1)],
                                                 in1=acc[:, t, r * H:(r + 1) * H], op0=ALU.mult, op1=ALU.add)
                ins.then_inc(acc_done, 1)

            def activations(i2, w):
                c = H if w else H // 2
                for h in range(2):
                    g_ps, u_ps = (bank[2 * h + n][:, :] if w else bank[n][:, h * c:(h + 1) * c] for n in range(2))
                    v.tensor_scalar(g_lim[h][:, 0:c], g_ps, LIMIT, None, ALU.min).then_inc(g_clamped, 1)
                    v.tensor_scalar(u_lim[h][:, 0:c], u_ps, LIMIT, -LIMIT, ALU.min, ALU.max).then_inc(u_clamped, 1)
                for h in range(2):
                    v.wait_ge(u_clamped, i2 + (h + 1))
                    v.wait_ge(g_clamped, i2 + (h + 1))
                    v.scalar_tensor_tensor(out=u_lim[h][:, 0:c], in0=u_lim[h][:, 0:c], scalar=1.0,
                                           in1=g_lim[h][:, 0:c], op0=ALU.add, op1=ALU.mult).then_inc(mid_act, 1)
                for h in range(2):
                    v.wait_ge(mid_act, i2 + (h + 1))
                    v.wait_ge(sig_ready, i2 + (h + 1))
                    v.tensor_tensor(act[:, h * c:(h + 1) * c], act[:, h * c:(h + 1) * c], u_lim[h][:, 0:c],
                                    ALU.mult).then_inc(act_ready, 1)

            def y_out(w):
                if w:
                    v.tensor_tensor(ysb[:, 0, :], bank[2][:, :], g2full[:, 0:H], ALU.mult)
                    v.tensor_tensor(ysb[:, 1, :], bank[3][:, :], g2full[:, H:], ALU.mult).then_inc(y_ready, 1)
                else:
                    v.tensor_tensor(ysb[:, 0, :], bank[2][:, :], g2half[:, :], ALU.mult).then_inc(y_ready, 1)

            def item(it, j, ws):
                i, i2 = it * UNROLL, it * (2 * UNROLL) + 2 * j
                ch = it * (UNROLL * NCH) + (CH_EXP + NCH * j)
                def select_next(w):
                    v.wait_ge(used, ch - 4)
                    select(i + (j + 1), 1 - j, w)

                either(v, ws[j + 2], select_next)
                for t in range(TT):
                    accumulate(i2, i + j, t)

                def middle(w):
                    v.wait_ge(used, ch + KT)
                    activations(i2, w)
                    v.wait_ge(used, ch + NCH)
                    y_out(w)

                either(v, ws[j + 1], middle)

            link(v.tensor_scalar(first[:, :], iota_e[:, :], -1.0, float(E), ALU.mult, ALU.add))
            link(v.tensor_tensor(first[:, :], first[:, :], over[:, :], ALU.mult))
            link(v.max(order[:, :], first[:, :]))
            v.tensor_scalar(eidx[:, :], order[0:1, :], -1.0, float(E), ALU.mult, ALU.add).then_inc(x_sp, 1)
            v.wait_ge(x_sp, 1)
            e0 = v.value_load(eidx[0:1, 0:1], min_val=0, max_val=E)
            step(v.tensor_scalar(slot[:, :, E:E + 1], slot[:, :, bass.ds(e0, 1)], float(-WIDE), None, ALU.add))
            step(v.tensor_copy(bsel[:, E:E + 1], bsel[:, bass.ds(e0, 1)]))

            take_b2()
            v.wait_ge(dve, n[0])
            v.wait_ge(acc_done, 1)
            with v.Fori(0, E // UNROLL) as it:
                ws = widths(v, it)
                for j in range(UNROLL):
                    item(it, j, ws)
            for t in range(TT):
                accumulate(2 * E, E, t)
            more = v.value_load(extras[0:1, 0:1], min_val=0, max_val=EXTRA)
            with v.If(more > 0):
                with v.Fori(0, more) as i:
                    e = v.value_load(eidx[0:1, bass.ds(i, 1)], min_val=0, max_val=E - 1)
                    with v.If(i > 0):
                        select(e, 0, True, second=1)
                    v.wait_ge(used, i * NCH + (CH_EXP + E * NCH + KT))
                    activations(i * 2 + 2 * E, True)
                    v.wait_ge(used, i * NCH + (CH_EXP + E * NCH + NCH))
                    y_out(True)
                    for t in range(TT):
                        accumulate(i * 2 + (2 * E + 2), e + 1, t)
                    v.wait_ge(acc_done, i * 2 + (2 * E + 5))
                    v.tensor_copy(most[:, :], eps[:, :]).then_inc(x_sel, 1)
                    v.wait_ge(x_sel, i + 1)
            with v.Else():
                v.wait_ge(acc_done, 2 * E + 3)
            v.tensor_copy(frstd[:, 0:1], eps[:, :]).then_inc(s_sum, 1)
            v.wait_ge(s_fng, 16)
            for t in range(TT):
                v.wait_ge(s_fr, t + 1)
                v.reciprocal(frstd[:, t:t + 1], fin[:, t:t + 1]).then_inc(s_ff, 1)
                v.wait_ge(s_ff, t + 1)
                v.scalar_tensor_tensor(out=acc[:, t, :], in0=acc[:, t, :], scalar=frstd[:, t:t + 1], in1=fng,
                                       op0=ALU.mult, op1=ALU.mult).then_inc(s_fin, 1)

        @block.tensor
        def _(pe):
            mm, tr = pe.matmul, pe.transpose
            pe.wait_ge(s_const, 7)
            pe.wait_ge(s_vec, 16 * 9)
            tr(bank[0][:, 0:120], vrow[0:120, :], ident[0:120, 0:120]).then_inc(p_vec, 1)
            pe.wait_ge(s_dw, 16)
            for k in range(KT):
                ins = tr(bank[1][:, k * TAPS:(k + 1) * TAPS], dwrow[:, k * P:(k + 1) * P], ident[0:TAPS, 0:TAPS])
            ins.then_inc(p_dw, 1)
            pe.wait_ge(s_x, 16)
            for k in range(KT):
                for t in range(TT):
                    ins = tr(bank[2 + k // 2][:, (k % 2) * T + t * P:(k % 2) * T + (t + 1) * P],
                             acc[:, t, k * P:(k + 1) * P], ident[:, :])
                if k % 2:
                    ins.then_inc(p_x, 1)

            def mean(b, src, k):
                return mm(bank[b][:, 0:T], mean_of[:, :], src[:, k, :], start=(k == 0), stop=(k == KT - 1))

            pe.wait_ge(s_const_v, 1)
            for k in range(KT):
                if k % 4 == 0:
                    pe.wait_ge(s_sq, k // 4 + 1)
                ins = mean(6, scratch, k)
            ins.then_inc(p_st, 1)

            def ada(kk):
                g, k = kk // KT, kk % KT
                n = number["ada", kk]
                pe.wait_ge(*chunk_in(n))
                if k == 0 and g:
                    pe.wait_ge(s_row, g)
                for j in range(4):
                    ins = mm(bank[7][32 * j:32 * j + 32, :], cwide[:, k, :], w_slot(n)[:, 512 * j:512 * j + 512],
                             start=(k == 0), stop=(k == KT - 1))
                ins.then_inc(used, 1)

            def turn_row(g):
                pe.wait_ge(s_row, g + 1)
                if g:
                    pe.wait_ge(s_mod, g)
                for q in range(4):
                    ins = tr(bank[0][:, q * P:(q + 1) * P], modrow[:, q * P:(q + 1) * P], ident[:, :])
                ins.then_inc(p_row, 1)

            pe.wait_ge(s_cwide, 1)
            pe.wait_ge(v_vec, 1)
            pe.wait_ge(v_dw, 1)
            for k in range(KT):
                ada(k)
            turn_row(0)

            def taps(t):
                pe.wait_ge(s_u, t + 1)
                pe.wait_ge(s_diag, diags_to[t])
                if t >= 2:
                    pe.wait_ge(s_conv, t - 1)
                last = share(t)[0] - 1
                for m in range(last + 1):
                    ins = mm(bank[3 + t % 2][:, 0:T], diag[:, (t % 2) * PE_TAPS + m, :], upad[:, t, m:m + T],
                             start=(m == 0), stop=(m == last))
                ins.then_inc(p_taps, 1)

            for t in range(KT):
                n = number["pw1", t]
                pe.wait_ge(*chunk_in(n))
                w = w_slot(n).rearrange("p (h k n) -> p h k n", h=2, k=KT)
                if t >= 2:
                    pe.wait_ge(s_u, t - 1)
                for h in range(2):
                    for k in range(KT):
                        if t == 0 and h == 0:
                            pe.wait_ge(s_h, k + 1)
                        ins = mm(bank[1 + t % 2][:, h * T:(h + 1) * T], w[:, h, k, :], hT[:, k, :],
                                 start=(k == 0), stop=(k == KT - 1))
                ins.then_inc(used, 1)
                if t:
                    taps(t - 1)
            for k in range(8):
                ada(KT + k)
            taps(KT - 1)
            for k in range(8, KT):
                ada(KT + k)
            for k in range(KT):
                pe.wait_ge(s_conv, k + 1)
                ins = mean(5, conv, k)
            ins.then_inc(p_st, 1)
            turn_row(1)
            for k in range(4):
                ada(2 * KT + k)
            pe.wait_ge(s_root, 1)
            for k in range(KT):
                pe.wait_ge(s_sq, 2 + k // 2 + 1)
                ins = mean(6, scratch, k)
            ins.then_inc(p_st, 1)
            for k in range(4, KT):
                ada(2 * KT + k)
            for m in range(KT):
                if m == 2:
                    turn_row(2)
                    pe.wait_ge(s_root, 2)
                    for r in range(2):
                        ins = mm(bank[6 + r][:, :], pick[:, r, :], modrow, start=True, stop=True)
                    ins.then_inc(p_g2, 1)
                n = number["pw2", m // 2]
                if m % 2 == 0:
                    pe.wait_ge(*chunk_in(n))
                w = w_slot(n).rearrange("p (k n) -> p k n", k=KT)
                if m >= 4:
                    pe.wait_ge(s_y2, m - 3)
                for k in range(KT):
                    if m == 0:
                        pe.wait_ge(s_silu, k + 1)
                    ins = mm(bank[1 + m % 4][:, 0:T], w[:, k, (m % 2) * P:(m % 2 + 1) * P], conv[:, k, :],
                             start=(k == 0), stop=(k == KT - 1))
                ins.then_inc(used if m % 2 else p_pw2, 1)
            pe.wait_ge(s_cent, 4)
            for k in range(KT):
                pe.wait_ge(s_sq, 6 + k + 1)
                ins = mean(5, scratch, k)
            ins.then_inc(p_st, 1)
            for b in range(4):
                t, d0 = b // 2, (b % 2) * 4
                for k in range(4):
                    ins = tr(bank[1 + b][:, k * P:(k + 1) * P], xT[:, d0 + k, t * P:(t + 1) * P], ident[:, :])
                ins.then_inc(p_x2, 1)
            pe.wait_ge(s_rw, 32)
            for k in range(KT):
                pe.wait_ge(s_h2v if k % 2 else s_h2, k // 2 + 1)
                ins = mm(bank[6][0:E, 0:T], rw[:, k, :], hT[:, k, :], start=(k == 0), stop=(k == KT - 1))
            ins.then_inc(p_log, 1)
            pe.wait_ge(s_logT, 1)
            for t in range(TT):
                ins = tr(bank[7][:, t * E:(t + 1) * E], logT[:, t * P:(t + 1) * P], ident[0:E, 0:E])
            ins.then_inc(p_log2, 1)
            for b in range(4):
                t, d0 = b // 2, (b % 2) * 4
                pe.wait_ge(s_x2c, b + 1)
                for k in range(4):
                    ins = tr(bank[1 + b][:, k * P:(k + 1) * P], hT[:, d0 + k, t * P:(t + 1) * P], ident[:, :])
                ins.then_inc(p_h2, 1)
            pe.wait_ge(s_mask, 1)
            pos = bank[0]
            mm(pos[:, 0:E], before[:, :], mask_bf[:, 0, :], start=True, stop=True)
            mm(pos[:, E:2 * E], ones_bf[:, :], mask_bf[:, 0, :], start=True, stop=False)
            mm(pos[:, E:2 * E], before[:, :], mask_bf[:, 1, :], start=False, stop=True)
            mm(pos[:, 2 * E:3 * E], ones_bf[:, :], mask_bf[:, 0, :], start=True, stop=False)
            mm(pos[:, 2 * E:3 * E], ones_bf[:, :], mask_bf[:, 1, :], start=False, stop=True).then_inc(p_pos, 1)
            def turn_onehot(b):
                for t in range(TT):
                    ins = tr(bank[6][:, t * P:(t + 1) * P], onehot[:, b, t, :], ident[:, :])
                ins.then_inc(oT_done, 1)

            def gather(b, w):
                m = WIDE if w else NARROW
                per = 512 // m
                for k in range(KT):
                    for part in range(3):
                        for t in range(TT):
                            ins = mm(bank[4 + k // per][:, k % per * m:(k % per + 1) * m],
                                     hsplit[:, part, t, k * P:(k + 1) * P], onehot_bf[:, b, t, 0:m],
                                     start=(part == 0 and t == 0), stop=(part == 2 and t == TT - 1))
                ins.then_inc(xg_done, 1)

            def scatter(b, w):
                for t in range(TT):
                    for r in range(2):
                        if w:
                            ins = mm(S_PS[t][r][:, :], onehotT[:, b, t, :], ysb[:, r, :], start=True, stop=True)
                        else:
                            ins = mm(S_PS[t][r][:, :], onehotT[64 * r:64 * r + 64, b, t, :],
                                     ysb[64 * r:64 * r + 64, 0, :], start=True, stop=True)
                    ins.then_inc(sc_done, 1)

            def arrived(i, q):
                pe.wait_ge(landed[q], i * 16 + 16 * (CH_EXP // RING + 1))
                return w_slot(q)

            def up_bias(b, w):
                for n in range(2):
                    for h in range(2):
                        m, dst = (WIDE, bank[2 * h + n][:, :]) if w else (NARROW, bank[n][64 * h:64 * h + 64, :])
                        mm(dst, bias_of[:, b, 0:m], b1s[:, n * F + h * H:n * F + (h + 1) * H],
                           start=True, stop=False)

            def up(i, b, w, ks):
                for k in ks:
                    wk = arrived(i, k)
                    for n in range(2):
                        for h in range(2):
                            m, dst = (WIDE, bank[2 * h + n][:, :]) if w else (NARROW, bank[n][64 * h:64 * h + 64, :])
                            ins = mm(dst, xg[:, b, k, 0:m], wk[:, n * F + h * H:n * F + (h + 1) * H],
                                     start=False, stop=(k == KT - 1))
                    ins.then_inc(used, 1)

            def down(i, i2, w):
                q = 4 if w else 2
                for h in range(2):
                    pe.wait_ge(act_ready, i2 + (h + 1))
                    for n in range(q):
                        ins = tr(bank[5 - h][:, n * P:(n + 1) * P], act[:, (h * q + n) * P:(h * q + n + 1) * P],
                                 ident[:, :])
                    ins.then_inc(aT_done, 1)
                pe.wait_ge(aT_ready, i2 + 1)
                for f in range(KT):
                    if f == q:
                        pe.wait_ge(aT_ready, i2 + 2)
                    wk = arrived(i, KT + f // 2) if f % 2 == 0 else wk
                    for r in range(2):
                        if w:
                            dst, lhsT = bank[2 + r][:, :], actT[:, f, :]
                        else:
                            dst, lhsT = bank[2][64 * r:64 * r + 64, :], actT[:, f % 4, 64 * (f // 4):64 * (f // 4) + 64]
                        ins = mm(dst, lhsT, wk[:, f % 2 * D + r * H:f % 2 * D + (r + 1) * H],
                                 start=(f == 0), stop=(f == KT - 1))
                    if f % 2:
                        ins.then_inc(used, 1)

            def item(it, j, ws):
                i, i2, b = it * UNROLL, it * (2 * UNROLL) + 2 * j, j
                i = i + j
                pe.wait_ge(xg_ready, i + 1)
                pe.wait_ge(oT_ready, i + 1)

                def first(w):
                    if w:
                        pe.wait_ge(y_ready, i + 1)
                    up_bias(b, w)
                    up(i, b, w, range(2))

                either(pe, ws[j + 1], first)
                pe.wait_ge(y_ready, i + 1)
                pe.wait_ge(acc_done, i2 + 1)
                either(pe, ws[j], lambda w: scatter(1 - b, w))
                either(pe, ws[j + 1], lambda w: up(i, b, w, range(2, KT)))
                pe.wait_ge(sel_ready, i * 5 + 10)
                pe.wait_ge(acc_done, i2 + 3)
                either(pe, ws[j + 2], lambda w: gather(1 - b, w))
                turn_onehot(1 - b)
                pe.wait_ge(xg_ready, i + 2)
                either(pe, ws[j + 1], lambda w: down(i, i2, w))

            pe.wait_ge(s_tab, 1)
            w0 = pe.value_load(wide[0:1, 1:2], min_val=0, max_val=1)
            pe.wait_ge(sel_ready, 5)
            turn_onehot(0)
            pe.wait_ge(s_lo, 2)
            pe.wait_ge(s_lov, 2)
            either(pe, w0, lambda w: gather(0, w))
            pe.wait_ge(s_gate, TT)
            for t in range(TT):
                ins = tr(bank[7][:, t * P:(t + 1) * P], gate4[:, t, :, :].rearrange("p r e -> p (r e)"), ident[:, :])
            ins.then_inc(p_gT, 1)
            pe.wait_ge(s_gT, 1)
            pe.wait_ge(s_b2g, 1)
            pe.wait_ge(oT_ready, 1)
            pe.wait_ge(xg_ready, 1)
            for r in range(2):
                for t in range(TT):
                    g = (2 * r + t) * E
                    ins = mm(S_PS[t][r][:, :], gateT4[g:g + E, t * P:(t + 1) * P], b2g[g:g + E, :],
                             start=True, stop=True)
            ins.then_inc(p_b2, 1)
            with pe.Fori(0, E // UNROLL) as it:
                ws = widths(pe, it)
                for j in range(UNROLL):
                    item(it, j, ws)
            wl = pe.value_load(wide[0:1, E:E + 1], min_val=0, max_val=1)
            pe.wait_ge(y_ready, E + 1)
            pe.wait_ge(oT_ready, E + 1)
            pe.wait_ge(xg_ready, E + 1)
            pe.wait_ge(acc_done, 2 * E + 1)
            either(pe, wl, lambda w: scatter(1, w))
            more = pe.value_load(extras[0:1, 0:1], min_val=0, max_val=EXTRA)
            with pe.If(more > 0):
                with pe.Fori(0, more) as i:
                    with pe.If(i > 0):
                        pe.wait_ge(sel_ready, i * 5 + 5 * (E + 1))
                        pe.wait_ge(acc_done, i * 2 + (2 * E + 3))
                        turn_onehot(0)
                        gather(0, True)
                    pe.wait_ge(xg_ready, i + (E + 1))
                    pe.wait_ge(y_ready, i + (E + 1))
                    up_bias(0, True)
                    up(i + E, 0, True, range(KT))
                    pe.wait_ge(acc_done, i * 2 + (2 * E + 3))
                    down(i + E, i * 2 + 2 * E, True)
                    pe.wait_ge(y_ready, i + (E + 2))
                    pe.wait_ge(oT_ready, i + (E + 1))
                    scatter(0, True)


_INS = ["x", "c", "ada_w", "ada_b", "mix_norm_g", "ffn_norm_g", "conf_pw1_w", "conf_pw1_b", "conf_dw_w",
        "conf_dw_b", "conf_ln_g", "conf_ln_b", "conf_pw2_w", "conf_pw2_b", "router_w", "router_b",
        "exp_w1", "exp_b1", "exp_w2", "exp_b2", "final_norm_g"]


def kernel(**inputs):
    import numpy as np
    import concourse.bacc as bacc
    from concourse.bass_utils import run_bass_kernel_spmd

    nc = bacc.Bacc("TRN2", target_bir_lowering=False, num_devices=1)
    arrays, args = {}, []
    for name in _INS:
        arr = np.ascontiguousarray(inputs[name])
        arrays[f"in_{name}"] = arr
        args.append(nc.dram_tensor(f"in_{name}", arr.shape, mybir.dt.from_np(arr.dtype), kind="ExternalInput").ap())
    out = nc.dram_tensor("out", inputs["x"].shape, F32, kind="ExternalOutput").ap()
    build_trunk(nc, *args, out)
    r = run_bass_kernel_spmd(nc, [arrays], core_ids=[0])
    return r.results[0]["out"]
```
